# Optimizing a Trainium2 kernel written in Bass

```python
import math
import jax
import jax.numpy as jnp
from jax import lax
import numpy as np

D_MODEL = 1024
BATCH = 1
SEQ = 2048
DEPTH = 1

N_MIXERS = 3
N_CONV_LAYERS = len(range(0, DEPTH, N_MIXERS))
N_NSA_LAYERS = len(range(1, DEPTH, N_MIXERS))
N_MLA_LAYERS = len(range(2, DEPTH, N_MIXERS))

EPS = 1e-6
NEG = -1e30
BIG = 1e30
ROPE_THETA = 500000.0

CONV_WIDTH = 31

NSA_HEADS = 16
NSA_KV_GROUPS = 4
NSA_HEAD_DIM = D_MODEL // NSA_HEADS
NSA_ROT_DIM = NSA_HEAD_DIM // 4
CMP_BLOCK = 32
CMP_STRIDE = 16
SLC_BLOCK = 64
SLC_TOP_N = 16
WINDOW = 512
NSA_Q_BLOCK = 64
NSA_Q_DIM = NSA_HEADS * NSA_HEAD_DIM
NSA_KV_DIM = NSA_KV_GROUPS * NSA_HEAD_DIM
NSA_SIZES = [NSA_Q_DIM] + [NSA_KV_DIM] * 6 + [3 * NSA_HEADS]
NSA_IN = sum(NSA_SIZES)
NSA_SPLITS = [int(v) for v in np.cumsum(NSA_SIZES)[:-1]]

MLA_HEADS = 16
MLA_Q_LORA = 384
MLA_KV_LORA = 256
MLA_NOPE = 64
MLA_ROPE = 32
MLA_V = 64
MLA_QK = MLA_NOPE + MLA_ROPE
MLA_IN = MLA_Q_LORA + MLA_KV_LORA + MLA_ROPE
MLA_Q_BLOCK = 128

N_EXPERTS = 16
N_GROUPS = 4
EXPERTS_PER_GROUP = N_EXPERTS // N_GROUPS
TOP_K = 2
D_EXPERT = 512

kernel_name = "hybrid_conv_nsa_mla_grouped_moe"

def rms_norm(x, g):
    xf = x.astype(jnp.float32)
    y = xf * lax.rsqrt(jnp.mean(xf * xf, axis=-1, keepdims=True) + EPS)
    return (y * g.astype(jnp.float32)).astype(x.dtype)

def layer_norm(x, g, b):
    xf = x.astype(jnp.float32)
    mu = jnp.mean(xf, axis=-1, keepdims=True)
    var = jnp.mean(jnp.square(xf - mu), axis=-1, keepdims=True)
    y = (xf - mu) * lax.rsqrt(var + EPS) * g.astype(jnp.float32) + b.astype(jnp.float32)
    return y.astype(x.dtype)

def modulate(h, shift, scale):
    return h * (1.0 + scale[:, None, :]) + shift[:, None, :]

def rope_tables(pos, dim):
    inv_freq = ROPE_THETA ** (-jnp.arange(0, dim, 2, dtype=jnp.float32) / dim)
    ang = pos.astype(jnp.float32)[:, None] * inv_freq[None, :]
    return jnp.cos(ang)[:, None, :], jnp.sin(ang)[:, None, :]

def apply_rope(x, cos, sin):
    x1, x2 = jnp.split(x.astype(jnp.float32), 2, axis=-1)
    return jnp.concatenate([x1 * cos - x2 * sin, x2 * cos + x1 * sin], axis=-1).astype(x.dtype)

def partial_rope(x, cos, sin, rot):
    return jnp.concatenate([apply_rope(x[..., :rot], cos, sin), x[..., rot:]], axis=-1)

def conv_mixer(h, w_pw1, b_pw1, w_dw, b_dw, ln_g, ln_b, w_pw2, b_pw2):
    a, g = jnp.split(h @ w_pw1 + b_pw1, 2, axis=-1)
    u = a * jax.nn.sigmoid(g)
    u = jnp.pad(u, ((0, 0), (CONV_WIDTH - 1, 0), (0, 0)))
    u = lax.conv_general_dilated(u, w_dw[:, None, :], window_strides=(1,), padding='VALID',
                                 dimension_numbers=('NWC', 'WIO', 'NWC'),
                                 feature_group_count=D_MODEL) + b_dw
    u = layer_norm(u, ln_g, ln_b)
    return jax.nn.silu(u) @ w_pw2 + b_pw2

def nsa_mixer(h, w_in, w_cmp1, w_cmp2, cmp_pos, q_gain, k_gain, w_out):
    B, S, _ = h.shape
    H, G, dh = NSA_HEADS, NSA_KV_GROUPS, NSA_HEAD_DIM
    R = H // G
    n_cmp = S // CMP_STRIDE - 1
    n_slc = S // SLC_BLOCK
    n_top = min(SLC_TOP_N, n_slc)
    QB = NSA_Q_BLOCK
    scale = dh ** -0.5
    cos, sin = rope_tables(jnp.arange(S), NSA_ROT_DIM)
    cmp_end = jnp.arange(n_cmp) * CMP_STRIDE + (CMP_BLOCK - 1)
    cos_c, sin_c = rope_tables(cmp_end, NSA_ROT_DIM)

    q, kc, vc, ks, vs, kw, vw, gl = jnp.split(h @ w_in, NSA_SPLITS, axis=-1)
    q = partial_rope(rms_norm(q.reshape(B, S, H, dh), q_gain), cos, sin, NSA_ROT_DIM)

    def kv(t):
        return t.reshape(B, S, G, dh)

    def compress(t, w1, w2, pe):
        tr = t.reshape(B, S // CMP_STRIDE, CMP_STRIDE, G, dh)
        blk = jnp.concatenate([tr[:, :-1], tr[:, 1:]], axis=2) + pe[:, None, :]
        z = jax.nn.silu(jnp.einsum('bnlgd,lde->bnge', blk, w1))
        return jnp.einsum('bnge,ef->bngf', z, w2)

    kc = compress(kv(kc), w_cmp1[0], w_cmp2[0], cmp_pos[0])
    vc = compress(kv(vc), w_cmp1[1], w_cmp2[1], cmp_pos[1])
    kc = partial_rope(rms_norm(kc, k_gain[0]), cos_c, sin_c, NSA_ROT_DIM)
    ks = partial_rope(rms_norm(kv(ks), k_gain[1]), cos, sin, NSA_ROT_DIM)
    kw = partial_rope(rms_norm(kv(kw), k_gain[2]), cos, sin, NSA_ROT_DIM)

    def hf(t):
        return t.transpose(0, 2, 1, 3)

    qg = hf(q).reshape(B, G, R, S, dh)
    kc, vc = hf(kc), hf(vc)
    ks_blk = hf(ks).reshape(B, G, n_slc, SLC_BLOCK, dh)
    vs_blk = hf(kv(vs)).reshape(B, G, n_slc, SLC_BLOCK, dh)
    pad = ((0, 0), (0, 0), (WINDOW, 0), (0, 0))
    kw_pad = jnp.pad(hf(kw), pad)
    vw_pad = jnp.pad(hf(kv(vw)), pad)
    gates = jax.nn.sigmoid(gl.astype(jnp.float32)).reshape(B, S, H, 3)
    gates = gates.transpose(0, 2, 1, 3).reshape(B, G, R, S, 3)

    ii = jnp.arange(n_cmp)[:, None]
    jj = jnp.arange(n_slc)[None, :]
    overlap = ((ii * CMP_STRIDE < (jj + 1) * SLC_BLOCK) &
               (ii * CMP_STRIDE + CMP_BLOCK > jj * SLC_BLOCK)).astype(jnp.float32)
    bi = jnp.arange(B)[:, None, None, None]
    gi = jnp.arange(G)[None, :, None, None]
    slot = jnp.arange(SLC_BLOCK)
    blk_id = jnp.arange(n_slc)

    def q_block(qi):
        t0 = qi * QB
        tq = t0 + jnp.arange(QB)
        qb = lax.dynamic_slice_in_dim(qg, t0, QB, axis=3)
        gb = lax.dynamic_slice_in_dim(gates, t0, QB, axis=3)
        s = jnp.einsum('bgrqd,bgnd->bgrqn', qb, kc, preferred_element_type=jnp.float32) * scale
        m = cmp_end[None, :] <= tq[:, None]
        p = jnp.where(m, jax.nn.softmax(jnp.where(m, s, NEG), axis=-1), 0.0)
        o_c = jnp.einsum('bgrqn,bgnd->bgrqd', p.astype(vc.dtype), vc)
        imp = jnp.einsum('bgrqn,nj->bgqj', p, overlap)
        imp = jnp.where(blk_id[None, :] * SLC_BLOCK <= tq[:, None], imp, -BIG)
        forced = (blk_id[None, :] == 0) | (blk_id[None, :] == tq[:, None] // SLC_BLOCK)
        imp = jnp.where(forced, BIG, imp)
        _, sel = lax.top_k(imp, n_top)
        k_sel = ks_blk[bi, gi, sel].reshape(B, G, QB, n_top * SLC_BLOCK, dh)
        v_sel = vs_blk[bi, gi, sel].reshape(B, G, QB, n_top * SLC_BLOCK, dh)
        kpos = (sel[..., None] * SLC_BLOCK + slot).reshape(B, G, QB, n_top * SLC_BLOCK)
        s = jnp.einsum('bgrqd,bgqkd->bgrqk', qb, k_sel, preferred_element_type=jnp.float32) * scale
        m = (kpos <= tq[:, None])[:, :, None]
        p = jax.nn.softmax(jnp.where(m, s, NEG), axis=-1)
        o_s = jnp.einsum('bgrqk,bgqkd->bgrqd', p.astype(v_sel.dtype), v_sel)
        k_w = lax.dynamic_slice_in_dim(kw_pad, t0, QB + WINDOW, axis=2)
        v_w = lax.dynamic_slice_in_dim(vw_pad, t0, QB + WINDOW, axis=2)
        kpos_w = t0 - WINDOW + jnp.arange(QB + WINDOW)
        m = ((kpos_w[None, :] >= 0) & (kpos_w[None, :] <= tq[:, None]) &
             (kpos_w[None, :] > tq[:, None] - WINDOW))
        s = jnp.einsum('bgrqd,bgkd->bgrqk', qb, k_w, preferred_element_type=jnp.float32) * scale
        p = jax.nn.softmax(jnp.where(m, s, NEG), axis=-1)
        o_w = jnp.einsum('bgrqk,bgkd->bgrqd', p.astype(v_w.dtype), v_w)
        o = gb[..., 0:1] * o_c + gb[..., 1:2] * o_s + gb[..., 2:3] * o_w
        return o.astype(h.dtype)

    o = lax.map(q_block, jnp.arange(S // QB))
    o = o.transpose(1, 0, 4, 2, 3, 5).reshape(B, S, H * dh)
    return o @ w_out

def mla_mixer(h, w_in, q_lat_g, kv_lat_g, w_uq, w_ukv, q_gain, k_gain, w_out):
    B, S, _ = h.shape
    H = MLA_HEADS
    QB = MLA_Q_BLOCK
    scale = MLA_QK ** -0.5
    cos, sin = rope_tables(jnp.arange(S), MLA_ROPE)
    q_lat, kv_lat, k_pe = jnp.split(h @ w_in, [MLA_Q_LORA, MLA_Q_LORA + MLA_KV_LORA], axis=-1)
    q = (rms_norm(q_lat, q_lat_g) @ w_uq).reshape(B, S, H, MLA_QK)
    kvu = (rms_norm(kv_lat, kv_lat_g) @ w_ukv).reshape(B, S, H, MLA_NOPE + MLA_V)
    k_nope, v = jnp.split(kvu, [MLA_NOPE], axis=-1)
    k = jnp.concatenate([k_nope, jnp.broadcast_to(k_pe[:, :, None, :], (B, S, H, MLA_ROPE))], axis=-1)

    def norm_rot(t, g):
        t = rms_norm(t, g)
        return jnp.concatenate([t[..., :MLA_NOPE], apply_rope(t[..., MLA_NOPE:], cos, sin)], axis=-1)

    q = norm_rot(q, q_gain).transpose(0, 2, 1, 3)
    k = norm_rot(k, k_gain).transpose(0, 2, 1, 3)
    v = v.transpose(0, 2, 1, 3)
    kpos = jnp.arange(S)

    def q_block(qi):
        t0 = qi * QB
        qb = lax.dynamic_slice_in_dim(q, t0, QB, axis=2)
        s = jnp.einsum('bhqd,bhkd->bhqk', qb, k, preferred_element_type=jnp.float32) * scale
        m = kpos[None, :] <= (t0 + jnp.arange(QB))[:, None]
        p = jax.nn.softmax(jnp.where(m, s, NEG), axis=-1)
        return jnp.einsum('bhqk,bhkd->bhqd', p.astype(v.dtype), v)

    o = lax.map(q_block, jnp.arange(S // QB))
    o = o.transpose(1, 0, 3, 2, 4).reshape(B, S, H * MLA_V)
    return o @ w_out

def grouped_moe(h, router_w, router_bias, w_in, w_out):
    B, S, D = h.shape
    xt = h.reshape(-1, D)
    scores = jax.nn.sigmoid((xt @ router_w).astype(jnp.float32))
    biased = scores + router_bias.astype(jnp.float32)
    grp_score = lax.top_k(biased.reshape(-1, N_GROUPS, EXPERTS_PER_GROUP), 2)[0].sum(-1)
    g_sel = jnp.argmax(grp_score, axis=-1)
    expert_group = jnp.arange(N_EXPERTS) // EXPERTS_PER_GROUP
    masked = jnp.where(expert_group[None, :] == g_sel[:, None], biased, -BIG)
    _, expert = lax.top_k(masked, TOP_K)
    w = jnp.take_along_axis(scores, expert, axis=1)
    w = w / jnp.sum(w, axis=-1, keepdims=True)
    flat_e = expert.reshape(-1)
    order = jnp.argsort(flat_e)
    tok = order // TOP_K
    sizes = jnp.bincount(flat_e, length=N_EXPERTS).astype(jnp.int32)
    xs = xt[tok]
    gate, up = jnp.split(lax.ragged_dot(xs, w_in, sizes), 2, axis=-1)
    y = lax.ragged_dot(jax.nn.silu(gate) * up, w_out, sizes)
    y = y * w.reshape(-1)[order][:, None].astype(y.dtype)
    return jnp.zeros_like(xt).at[tok].add(y).reshape(B, S, D)

def setup_inputs(seed: int = 0) -> dict:
    key = jax.random.key(seed)
    keys = iter(jax.random.split(key, 48))

    def nrm(shape, scale):
        return jax.random.normal(next(keys), shape, jnp.float32) * scale

    def gain(shape):
        return 1.0 + nrm(shape, 0.02)

    D = D_MODEL
    NA, NB, NC = N_CONV_LAYERS, N_NSA_LAYERS, N_MLA_LAYERS
    dh = NSA_HEAD_DIM
    return {
        "x": nrm((BATCH, SEQ, D), 1.0),
        "c": nrm((BATCH, D), 1.0),
        "norm_mix_g": gain((DEPTH, D)),
        "norm_ffn_g": gain((DEPTH, D)),
        "w_ada": nrm((DEPTH, D, 6 * D), 0.5 * D ** -0.5),
        "b_ada": nrm((DEPTH, 6 * D), 0.02),
        "conv_w_pw1": nrm((NA, D, 2 * D), D ** -0.5),
        "conv_b_pw1": nrm((NA, 2 * D), 0.02),
        "conv_w_dw": nrm((NA, CONV_WIDTH, D), CONV_WIDTH ** -0.5),
        "conv_b_dw": nrm((NA, D), 0.02),
        "conv_ln_g": gain((NA, D)),
        "conv_ln_b": nrm((NA, D), 0.02),
        "conv_w_pw2": nrm((NA, D, D), D ** -0.5),
        "conv_b_pw2": nrm((NA, D), 0.02),
        "nsa_w_in": nrm((NB, D, NSA_IN), D ** -0.5),
        "nsa_w_cmp1": nrm((NB, 2, CMP_BLOCK, dh, dh), (CMP_BLOCK * dh) ** -0.5),
        "nsa_w_cmp2": nrm((NB, 2, dh, dh), dh ** -0.5),
        "nsa_cmp_pos": nrm((NB, 2, CMP_BLOCK, dh), 0.1),
        "nsa_q_gain": gain((NB, dh)),
        "nsa_k_gain": gain((NB, 3, dh)),
        "nsa_w_out": nrm((NB, NSA_Q_DIM, D), NSA_Q_DIM ** -0.5),
        "mla_w_in": nrm((NC, D, MLA_IN), D ** -0.5),
        "mla_q_lat_g": gain((NC, MLA_Q_LORA)),
        "mla_kv_lat_g": gain((NC, MLA_KV_LORA)),
        "mla_w_uq": nrm((NC, MLA_Q_LORA, MLA_HEADS * MLA_QK), MLA_Q_LORA ** -0.5),
        "mla_w_ukv": nrm((NC, MLA_KV_LORA, MLA_HEADS * (MLA_NOPE + MLA_V)), MLA_KV_LORA ** -0.5),
        "mla_q_gain": gain((NC, MLA_QK)),
        "mla_k_gain": gain((NC, MLA_QK)),
        "mla_w_out": nrm((NC, MLA_HEADS * MLA_V, D), (MLA_HEADS * MLA_V) ** -0.5),
        "router_w": nrm((D, N_EXPERTS), D ** -0.5),
        "router_bias": nrm((N_EXPERTS,), 0.01),
        "moe_w_in": nrm((DEPTH, N_EXPERTS, D, 2 * D_EXPERT), D ** -0.5),
        "moe_w_out": nrm((DEPTH, N_EXPERTS, D_EXPERT, D), D_EXPERT ** -0.5),
    }

def reference(x, c, norm_mix_g, norm_ffn_g, w_ada, b_ada,
              conv_w_pw1, conv_b_pw1, conv_w_dw, conv_b_dw, conv_ln_g, conv_ln_b, conv_w_pw2, conv_b_pw2,
              nsa_w_in, nsa_w_cmp1, nsa_w_cmp2, nsa_cmp_pos, nsa_q_gain, nsa_k_gain, nsa_w_out,
              mla_w_in, mla_q_lat_g, mla_kv_lat_g, mla_w_uq, mla_w_ukv, mla_q_gain, mla_k_gain, mla_w_out,
              router_w, router_bias, moe_w_in, moe_w_out):
    mods = jnp.einsum('bd,lde->lbe', jax.nn.silu(c), w_ada) + b_ada[:, None, :]
    for i in range(DEPTH):
        sh1, sc1, g1, sh2, sc2, g2 = jnp.split(mods[i], 6, axis=-1)
        h = modulate(rms_norm(x, norm_mix_g[i]), sh1, sc1)
        kind, j = i % N_MIXERS, i // N_MIXERS
        if kind == 0:
            y = conv_mixer(h, conv_w_pw1[j], conv_b_pw1[j], conv_w_dw[j], conv_b_dw[j],
                           conv_ln_g[j], conv_ln_b[j], conv_w_pw2[j], conv_b_pw2[j])
        elif kind == 1:
            y = nsa_mixer(h, nsa_w_in[j], nsa_w_cmp1[j], nsa_w_cmp2[j], nsa_cmp_pos[j],
                          nsa_q_gain[j], nsa_k_gain[j], nsa_w_out[j])
        else:
            y = mla_mixer(h, mla_w_in[j], mla_q_lat_g[j], mla_kv_lat_g[j], mla_w_uq[j],
                          mla_w_ukv[j], mla_q_gain[j], mla_k_gain[j], mla_w_out[j])
        x = x + g1[:, None, :] * y
        h = modulate(rms_norm(x, norm_ffn_g[i]), sh2, sc2)
        x = x + g2[:, None, :] * grouped_moe(h, router_w, router_bias, moe_w_in[i], moe_w_out[i])
    return x


_drawn_inputs = setup_inputs


def setup_inputs(seed=0):
    import zlib

    import numpy as np

    out = dict(_drawn_inputs(seed))
    spreads = {}
    factors = {'norm_mix_g': 4.349,
     'conv_b_pw1': 5.199,
     'conv_b_dw': 3.962,
     'conv_ln_g': 11.586,
     'conv_ln_b': 4.565,
     'conv_b_pw2': 3.403,
     'norm_ffn_g': 3.049}
    for name, (base, spread) in spreads.items():
        noise = np.random.default_rng([zlib.crc32(name.encode()), seed]).standard_normal(out[name].shape)
        drawn = base * np.exp(spread * noise) if base else spread * noise
        out[name] = jnp.asarray(drawn.astype(out[name].dtype))
    for name, factor in factors.items():
        out[name] = (out[name] * factor).astype(out[name].dtype)
    return out
```

```python
from contextlib import ExitStack

import concourse.bass as bass
from concourse import mybir

F32 = mybir.dt.float32
F16 = mybir.dt.float16
BF16 = mybir.dt.bfloat16
I32 = mybir.dt.int32
ALU = mybir.AluOpType
ACT = mybir.ActivationFunctionType
AX_X = mybir.AxisListType.X

P = 128
EPS = 1e-6
BIG = 1e30


def kernel_program(nc, x, c, norm_mix_g, norm_ffn_g, w_ada, b_ada, conv_w_pw1, conv_b_pw1, conv_w_dw,
                   conv_b_dw, conv_ln_g, conv_ln_b, conv_w_pw2, conv_b_pw2, router_w, router_bias,
                   moe_w_in, moe_w_out, out):
    _, S, D = x.shape
    KD = D // P
    TB = 512
    NB = S // TB
    TT = TB // P
    NT = S // P
    CW = conv_w_dw.shape[1]
    HIST = CW - 1
    NP = KD // 2
    E = router_w.shape[1]
    NG = 4
    EG = E // NG
    DE = moe_w_out.shape[2]
    KE = DE // P
    MT = 2 * S // P + E - 1
    MTP = MT + 1
    H = D // 2
    NPIECE = w_ada.shape[2] // H

    x1_dram = nc.dram_tensor("x1_scratch", (S, D), F32, kind="Internal").ap()
    h2_dram = nc.dram_tensor("h2_scratch", (S, D), F32, kind="Internal").ap()
    y_dram = nc.dram_tensor("y_scratch", (MT * P, D), F32, kind="Internal").ap()

    keep = ExitStack()
    with keep:
        def sem(name, ctx=keep):
            return ctx.enter_context(nc.semaphore(name))

        def sb(name, shape, dt=F32, ctx=keep):
            return ctx.enter_context(nc.sbuf_tensor(name, shape, dt))

        ident = sb("ident", [P, P])
        g2_row = sb("g2_row", [P, D])
        logits = sb("logits", [P, NT, E])
        bank = [keep.enter_context(nc.psum_tensor(f"bank{i}", [P, 512], F32)) for i in range(8)]

        conv = ExitStack()
        with conv:
            def cb(name, shape, dt=F32):
                return sb(name, shape, dt, conv)

            def cs(name):
                return sem(name, conv)

            ps_a, ps_g = [bank[0], bank[1]], [bank[2], bank[3]]
            ps_m, ps_y, ps_t = bank[4], bank[5], [bank[6], bank[7]]

            w1 = cb("w1", [P, 2, KD, 2, P])
            w2 = cb("w2", [P, KD, D])
            xt = cb("xt", [P, TT, D])
            hT = cb("hT", [P, KD, TB])
            u = cb("u", [P, KD, HIST + TB])
            v = cb("v", [P, KD, TB])
            s = cb("s", [P, KD, TB])
            ybuf = cb("ybuf", [P, TT, D])
            xr = cb("xr", [P, 2, D])
            h2 = cb("h2", [P, 2, D])
            h2T = cb("h2T", [P, KD, P])
            sig = cb("sig", [P, 2, TB])
            sq = cb("sq", [P, 2, TB])
            rstd = cb("rstd", [P, TB])
            eps_col = cb("eps_col", [P, 1])
            junk = cb("junk", [P, 2, D], BF16)
            gb_row = cb("gb_row", [P, D])
            G2_row = cb("G2_row", [P, D])
            sh2_row = cb("sh2_row", [P, D])
            ones_mean = cb("ones_mean", [P, P])
            ones_row = cb("ones_row", [1, P])
            vec_rows = cb("vec_rows", [7 * KD, P])
            vec = cb("vec", [P, 7 * KD])
            wdw_rows = cb("wdw_rows", [CW, D])
            wdw = cb("wdw", [P, KD, CW])
            csil = cb("csil", [P, KD])
            cols = cb("cols", [P, 2 * KD])
            rw = cb("rw", [P, KD, E])
            small = cb("small", [P, 8, TT])
            half = cb("half", [P, TT])

            V_NG, V_B1, V_BDW, V_LG, V_LB, V_C = 0, KD, 3 * KD, 4 * KD, 5 * KD, 6 * KD
            ada = [v, s]
            csil_bc = xr[:, 0, :].rearrange("p (k m) -> p k m", k=KD)
            bada = [h2[:, 1, i * H:(i + 1) * H] for i in range(2)]
            sh1_row, sc1_row = ybuf[:, 0, :], ybuf[:, 1, :]
            g1_row = ybuf[:, 2, :]
            b2_row, ng2_row = ybuf[:, 3, :], h2[:, 0, :]
            mod_rows = [sh1_row, sc1_row, g1_row, sh2_row[:], G2_row[:], g2_row[:]]
            ss1, r1, ss2, r2 = (small[:, i, :] for i in range(4))
            m1, m2 = small[:, 4, :], small[:, 5, :]

            consts = cs("consts")
            ident0 = cs("ident0")
            vec_in = cs("vec_in")
            w2_in = cs("w2_in")
            ada_in = [cs(f"ada_in{i}") for i in range(2)]
            pro_t = cs("pro_t")
            pro_v = cs("pro_v")
            pro_a = cs("pro_a")
            mods_full = cs("mods_full")
            mods_row = cs("mods_row")
            x_in = [cs(f"x_in{i}") for i in range(TT)]
            w1_in = [cs(f"w1_in{i}") for i in range(2)]
            xr_in = [cs(f"xr_in{i}") for i in range(2)]
            ss1_done, rstd1_done, xn_done = cs("ss1_done"), cs("rstd1_done"), cs("xn_done")
            ms1_done, ms2_done = cs("ms1_done"), cs("ms2_done")
            t_full = [cs(f"t_full{i}") for i in range(2)]
            t_free = [cs(f"t_free{i}") for i in range(2)]
            g_full, a_full = cs("g_full"), cs("a_full")
            sig_done, glu_done = cs("sig_done"), cs("glu_done")
            tap_done, hist_done = cs("tap_done"), cs("hist_done")
            mean_full, ln1_done = cs("mean_full"), cs("ln1_done")
            sq_done, var_step = cs("sq_done"), cs("var_step")
            std_done, rstd_done, ln2_done, silu_done = cs("std_done"), cs("rstd_done"), cs("ln2_done"), cs("silu_done")
            y_full, y_free = cs("y_full"), cs("y_free")
            x1_done, ss2_done, rstd2_done = cs("x1_done"), cs("ss2_done"), cs("rstd2_done")
            h2_half, h2_done = cs("h2_half"), cs("h2_done")
            x1_out = [cs(f"x1_out{i}") for i in range(TT)]
            h2_out = [cs(f"h2_out{i}") for i in range(2)]

            def before_x(b):
                if b < 2:
                    return 4 * b, 4 * b
                return 12 * b - 16, 8 * b - 8

            def before_router(q):
                absent = 4 * max(0, q + 3 - NB)
                return 12 * q + 12 - absent, 8 * q + 12 - absent

            def tile_rows(ap, b, i):
                return ap[b * TB + i * P:b * TB + (i + 1) * P, :]

            x_rows = x.rearrange("o s d -> (o s) d")

            block = conv.enter_context(nc.Block())

            def load_x(sp, b):
                for i in range(TT):
                    sp.dma_start(xt[:, i, :], tile_rows(x_rows, b, i)).then_inc(x_in[i], 16)

            def load_w1(sp, b, p):
                for cc in range(2):
                    if b or p:
                        sp.wait_ge(a_full, KD * b + 2 * p + cc - 1)
                    ch = 2 * p + cc
                    for ag in range(2):
                        col = ag * D + ch * P
                        sp.dma_start(w1[:, cc, :, ag, :], conv_w_pw1[0, :, col:col + P].rearrange(
                            "(k p) m -> p k m", p=P)).then_inc(w1_in[cc], 16)

            def load_xr(sp, q, tiles):
                for i in tiles:
                    if i >= 2:
                        sp.wait_ge(x1_done, TT * q + i - 1)
                    else:
                        sp.wait_ge(x1_done, TT * q)
                    sp.dma_start(xr[:, i % 2, :], tile_rows(x_rows, q, i)).then_inc(xr_in[i % 2], 16)

            def sp_block(sp, b, first=False, last=False):
                for p in range(1, NP):
                    load_w1(sp, b, p)
                    if p == 1 and not last:
                        sp.wait_ge(t_full[1], 4 * b + 4)
                        load_x(sp, b + 1)
                    if p == 2 and not first:
                        load_xr(sp, b - 1, (0, 1))
                if not last:
                    load_w1(sp, b + 1, 0)
                if not first:
                    load_xr(sp, b - 1, (2, 3))

            @block.sync
            def _(sp):
                vecs = [(norm_mix_g, V_NG, KD), (conv_b_pw1, V_B1, 2 * KD), (conv_b_dw, V_BDW, KD),
                        (conv_ln_g, V_LG, KD), (conv_ln_b, V_LB, KD), (c, V_C, KD)]
                for t, at, n in vecs:
                    sp.dma_start(vec_rows[at:at + n, :], t.rearrange("o (k p) -> (o k) p", p=P)).then_inc(vec_in, 16)
                sp.dma_start(wdw_rows[:], conv_w_dw[0]).then_inc(vec_in, 16)
                sp.dma_start(rw[:], router_w.rearrange("(k p) e -> p k e", p=P)).then_inc(vec_in, 16)
                sp.dma_start(b2_row, conv_b_pw2.to_broadcast([P, D])).then_inc(vec_in, 16)
                sp.dma_start(ng2_row, norm_ffn_g.to_broadcast([P, D])).then_inc(vec_in, 16)
                for j in range(NPIECE):
                    if j >= 2:
                        sp.wait_ge(mods_row, j - 1)
                    sp.dma_start(ada[j % 2][:], w_ada[0].rearrange("(k p) n -> p k n", p=P)[:, :, j * H:(j + 1) * H]).then_inc(ada_in[j % 2], 16)
                    sp.dma_start(bada[j % 2], b_ada[:, j * H:(j + 1) * H].to_broadcast([P, H])).then_inc(ada_in[j % 2], 16)
                    if j == 1:
                        load_x(sp, 0)
                sp.dma_start(w2[:], conv_w_pw2[0].rearrange("(k p) n -> p k n", p=P)).then_inc(w2_in, 16)
                load_w1(sp, 0, 0)
                for b in range(NB):
                    sp_block(sp, b, first=b == 0, last=b == NB - 1)
                load_xr(sp, NB - 1, range(TT))
                for i in range(TT):
                    sp.wait_ge(x1_out[i], 16 * NB)
                for i in range(2):
                    sp.wait_ge(h2_out[i], 16 * NB * TT // 2)

            def rstd_of_x(pool, b):
                pool.wait_ge(ss1_done, TT * (b + 1))
                pool.tensor_scalar(m1, ss1, 1.0 / D, EPS, ALU.mult, ALU.add).then_inc(ms1_done, 1)
                pool.wait_ge(ms1_done, b + 1)
                pool.wait_ge(xn_done, TT * b)
                pool.tensor_tensor(r1, m1, half[:], ALU.pow).then_inc(rstd1_done, 1)

            def pool_post(pool, q):
                for j in range(2):
                    for i in (2 * j, 2 * j + 1):
                        pool.wait_ge(x1_done, TT * q + i + 1)
                        pool.dma_start(tile_rows(x1_dram, q, i), ybuf[:, i, :]).then_inc(x1_out[i], 16)
                    pool.wait_ge(ss2_done, TT * q + 2 * j + 2)
                    pair = slice(2 * j, 2 * j + 2)
                    pool.tensor_scalar(m2[:, pair], ss2[:, pair], 1.0 / D, EPS, ALU.mult, ALU.add).then_inc(ms2_done, 1)
                    pool.wait_ge(ms2_done, 2 * q + j + 1)
                    pool.wait_ge(h2_half, TT * q)
                    pool.tensor_tensor(r2[:, pair], m2[:, pair], half[:, pair], ALU.pow).then_inc(rstd2_done, 1)
                    for i in (2 * j, 2 * j + 1):
                        pool.wait_ge(h2_done, TT * q + i + 1)
                        pool.dma_start(tile_rows(h2_dram, q, i), h2[:, i % 2, :]).then_inc(h2_out[i % 2], 16)

            def pool_block(pool, b, first=False, last=False):
                if not last:
                    rstd_of_x(pool, b + 1)
                if not first:
                    pool_post(pool, b - 1)

            @block.gpsimd
            def _(pool):
                pool.memset(ident[:], 0.0).then_inc(ident0, 1)
                pool.wait_ge(ident0, 1)
                pool.affine_select(out=ident[:], in_=ident[:], compare_op=ALU.not_equal, fill=1.0, base=0,
                                   pattern=[[-1, P]], channel_multiplier=1).then_inc(consts, 1)
                pool.memset(ones_mean[:], 1.0 / D).then_inc(consts, 1)
                pool.memset(ones_row[:], 1.0).then_inc(consts, 1)
                pool.memset(half[:], -0.5).then_inc(consts, 1)
                pool.memset(u[:, :, 0:HIST], 0.0).then_inc(consts, 1)
                pool.wait_ge(consts, 5)
                rstd_of_x(pool, 0)
                for b in range(NB):
                    pool_block(pool, b, first=b == 0, last=b == NB - 1)
                pool_post(pool, NB - 1)

            def transpose_x(pe, b):
                pe.wait_ge(xn_done, TT * (b + 1))
                for k in range(KD):
                    n = before_x(b)[k % 2] + k // 2
                    if n:
                        pe.wait_ge(t_free[k % 2], n)
                    for i in range(TT):
                        last = pe.transpose(ps_t[k % 2][:, i * P:(i + 1) * P], xt[:, i, k * P:(k + 1) * P], ident[:])
                    last.then_inc(t_full[k % 2], 1)

            def pointwise1(pe, b, p):
                if p == 0:
                    for t in range(2):
                        pe.wait_ge(t_free[t], before_x(b)[t] + 4)
                for cc in range(2):
                    pe.wait_ge(w1_in[cc], 32 * (NP * b + p + 1))
                    if b or p:
                        pe.wait_ge(glu_done, KD * b + 2 * p + cc - 1)
                    for ps, ag, full in ((ps_g, 1, g_full), (ps_a, 0, a_full)):
                        for k in range(KD):
                            last = pe.matmul(ps[cc][:], w1[:, cc, k, ag, :], hT[:, k, :], start=(k == 0), stop=(k == KD - 1))
                        last.then_inc(full, 1)

            def mean(pe, b, p):
                pe.wait_ge(tap_done, 2 * CW * (NP * b + p + 1))
                for cc in range(2):
                    ch = 2 * p + cc
                    last = pe.matmul(ps_m[:], ones_mean[:], v[:, ch, :], start=(ch == 0), stop=(ch == KD - 1))
                if p == NP - 1:
                    last.then_inc(mean_full, 1)

            def variance(pe, q):
                pe.wait_ge(ln1_done, KD * (q + 1))
                for k in range(KD):
                    pe.wait_ge(sq_done, KD * q + k + 1)
                    pe.matmul(ps_m[:], ones_mean[:], sq[:, k % 2, :], start=(k == 0), stop=(k == KD - 1)).then_inc(var_step, 1)

            def pointwise2(pe, q, i):
                if i == 0:
                    pe.wait_ge(silu_done, KD * (q + 1))
                for h in range(2):
                    pe.wait_ge(y_free, 2 * TT * q + 2 * i + h)
                    cols_h = slice(h * H, (h + 1) * H)
                    for k in range(KD):
                        pe.matmul(ps_y[:], s[:, k, i * P:(i + 1) * P], w2[:, k, cols_h], start=(k == 0), stop=False)
                    pe.matmul(ps_y[:], ones_row[:], gb_row[0:1, cols_h], start=False, stop=True).then_inc(y_full, 1)

            def router(pe, q, i):
                n0, n1 = before_router(q)[0] + 2 * i, before_router(q)[1] + i
                pe.wait_ge(h2_done, TT * q + i + 1)
                for t, n in ((0, n0), (1, n1)):
                    pe.wait_ge(t_free[t], n)
                    for k in range(4):
                        at = (4 * t + k) * P
                        last = pe.transpose(ps_t[t][:, k * P:(k + 1) * P], h2[:, i % 2, at:at + P], ident[:])
                    last.then_inc(t_full[t], 1)
                pe.wait_ge(t_free[0], n0 + 1)
                pe.wait_ge(t_free[1], n1 + 1)
                for k in range(KD):
                    last = pe.matmul(ps_t[0][:, 0:E], h2T[:, k, :], rw[:, k, :], start=(k == 0), stop=(k == KD - 1))
                last.then_inc(t_full[0], 1)

            def pe_block(pe, b, first=False, last=False):
                q = b - 1
                pointwise1(pe, b, 1)
                if not first:
                    variance(pe, q)
                    pe.wait_ge(std_done, b)
                mean(pe, b, 0)
                pointwise1(pe, b, 2)
                if not first:
                    pointwise2(pe, q, 0)
                mean(pe, b, 1)
                pointwise1(pe, b, 3)
                if not first:
                    pointwise2(pe, q, 1)
                    pointwise2(pe, q, 2)
                mean(pe, b, 2)
                if not first:
                    pointwise2(pe, q, 3)
                if not last:
                    transpose_x(pe, b + 1)
                    pointwise1(pe, b + 1, 0)
                mean(pe, b, 3)
                if not first:
                    for i in range(TT):
                        router(pe, q, i)

            @block.tensor
            def _(pe):
                pe.wait_ge(consts, 3)
                pe.wait_ge(vec_in, 160)
                pe.transpose(ps_t[0][:, 0:7 * KD], vec_rows[:], ident[0:7 * KD, 0:7 * KD]).then_inc(pro_t, 1)
                for k in range(KD):
                    last = pe.transpose(ps_t[1][:, k * CW:(k + 1) * CW], wdw_rows[:, k * P:(k + 1) * P], ident[0:CW, 0:CW])
                last.then_inc(pro_t, 1)
                pe.wait_ge(pro_v, 3)
                for j in range(NPIECE):
                    pe.wait_ge(ada_in[j % 2], 32 * (j // 2 + 1))
                    if j >= 2:
                        pe.wait_ge(mods_row, j - 1)
                    for k in range(KD):
                        last = pe.matmul(ps_a[j % 2][:], csil_bc[:, k, :], ada[j % 2][:, k, :], start=(k == 0), stop=(k == KD - 1))
                    last.then_inc(mods_full, 1)
                    if j == 3:
                        pe.wait_ge(mods_row, 4)
                        for r, row in enumerate((sh1_row, sc1_row)):
                            for n in range(2):
                                if n or r:
                                    pe.wait_ge(pro_v, 3 + 2 * r + n)
                                for k in range(4):
                                    at = (4 * n + k) * P
                                    last = pe.transpose(ps_g[0][:, k * P:(k + 1) * P], row[:, at:at + P], ident[:])
                                last.then_inc(pro_t, 1)
                transpose_x(pe, 0)
                pe.wait_ge(mods_row, NPIECE)
                pe.wait_ge(pro_v, 7)
                pointwise1(pe, 0, 0)
                for b in range(NB):
                    pe_block(pe, b, first=b == 0, last=b == NB - 1)
                variance(pe, NB - 1)
                for i in range(TT):
                    pointwise2(pe, NB - 1, i)
                for i in range(TT):
                    router(pe, NB - 1, i)

            def squares_of_x(act, b):
                for i in range(TT):
                    act.wait_ge(x_in[i], 16 * (b + 1))
                    act.wait_ge(ss1_done, TT * b + i)
                    act.activation(junk[:, 0, :], xt[:, i, :], ACT.Square, accum_out=ss1[:, i:i + 1]).then_inc(ss1_done, 1)

            def scale_x(act, b):
                act.wait_ge(rstd1_done, b + 1)
                for i in range(TT):
                    act.activation(xt[:, i, :], xt[:, i, :], ACT.Copy, scale=r1[:, i:i + 1]).then_inc(xn_done, 1)

            def copy_h(act, b):
                for k in range(KD):
                    n = before_x(b)[k % 2] + k // 2
                    act.wait_ge(t_full[k % 2], n + 1)
                    act.activation(hT[:, k, :], ps_t[k % 2][:], ACT.Identity, bias=cols[:, k:k + 1],
                                   scale=cols[:, KD + k:KD + k + 1]).then_inc(t_free[k % 2], 1)

            def sigmoids(act, b, p):
                for cc in range(2):
                    ch = 2 * p + cc
                    act.wait_ge(g_full, KD * b + ch + 1)
                    if b or p:
                        act.wait_ge(glu_done, KD * b + ch - 1)
                    act.activation(sig[:, cc, :], ps_g[cc][:], ACT.Sigmoid,
                                   bias=vec[:, V_B1 + KD + ch:V_B1 + KD + ch + 1]).then_inc(sig_done, 1)

            def act_norm(act, q):
                for k in range(KD):
                    act.wait_ge(ln1_done, KD * q + k + 1)
                    act.wait_ge(var_step, KD * q + max(k - 1, 0))
                    act.activation(sq[:, k % 2, :], s[:, k, :], ACT.Square).then_inc(sq_done, 1)
                act.wait_ge(var_step, KD * (q + 1))
                act.wait_ge(ln2_done, KD * q)
                act.activation(rstd[:], ps_m[:], ACT.Sqrt, bias=eps_col[:]).then_inc(std_done, 1)

            def act_silu(act, q):
                for k in range(KD):
                    act.wait_ge(ln2_done, KD * q + k + 1)
                    act.activation(s[:, k, :], s[:, k, :], ACT.Silu, bias=vec[:, V_LB + k:V_LB + k + 1],
                                   scale=vec[:, V_LG + k:V_LG + k + 1]).then_inc(silu_done, 1)

            def copy_y(act, q, i):
                act.wait_ge(x1_out[i], 16 * q)
                act.wait_ge(h2_done, TT * q)
                for h in range(2):
                    act.wait_ge(y_full, 2 * TT * q + 2 * i + h + 1)
                    act.copy(ybuf[:, i, h * H:(h + 1) * H], ps_y[:]).then_inc(y_free, 1)

            def square_x1(act, q, i):
                act.wait_ge(x1_done, TT * q + i + 1)
                act.wait_ge(ms2_done, 2 * q)
                act.wait_ge(ss2_done, TT * q + i)
                act.activation(junk[:, 1, :], ybuf[:, i, :], ACT.Square, accum_out=ss2[:, i:i + 1]).then_inc(ss2_done, 1)

            def copy_router(act, q, i):
                n0, n1 = before_router(q)[0] + 2 * i, before_router(q)[1] + i
                for t, n in ((0, n0), (1, n1)):
                    act.wait_ge(t_full[t], n + 1)
                    act.copy(h2T[:, 4 * t:4 * t + 4, :].rearrange("p k m -> p (k m)"), ps_t[t][:]).then_inc(t_free[t], 1)
                act.wait_ge(t_full[0], n0 + 2)
                act.copy(logits[:, q * TT + i, :], ps_t[0][:, 0:E]).then_inc(t_free[0], 1)

            def act_block(act, b, first=False, last=False):
                q = b - 1
                if not first:
                    act_norm(act, q)
                sigmoids(act, b, 1)
                if not first:
                    act_silu(act, q)
                sigmoids(act, b, 2)
                if not first:
                    copy_y(act, q, 0)
                if not last:
                    squares_of_x(act, b + 1)
                    scale_x(act, b + 1)
                sigmoids(act, b, 3)
                if not first:
                    copy_y(act, q, 1)
                    copy_y(act, q, 2)
                    square_x1(act, q, 0)
                    square_x1(act, q, 1)
                    copy_y(act, q, 3)
                if not last:
                    copy_h(act, b + 1)
                if not first:
                    for i in range(2, TT):
                        square_x1(act, q, i)
                if not last:
                    sigmoids(act, b + 1, 0)
                if not first:
                    for i in range(TT):
                        copy_router(act, q, i)

            @block.scalar
            def _(act):
                act.wait_ge(pro_v, 1)
                act.activation(csil[:], vec[:, V_C:V_C + KD], ACT.Silu).then_inc(pro_a, 1)
                squares_of_x(act, 0)
                act.wait_ge(pro_v, 8)
                scale_x(act, 0)
                copy_h(act, 0)
                sigmoids(act, 0, 0)
                for b in range(NB):
                    act_block(act, b, first=b == 0, last=b == NB - 1)
                act_norm(act, NB - 1)
                act_silu(act, NB - 1)
                for i in range(TT):
                    copy_y(act, NB - 1, i)
                for i in range(TT):
                    square_x1(act, NB - 1, i)
                for i in range(TT):
                    copy_router(act, NB - 1, i)

            def glu(dve, b, p):
                if b:
                    dve.wait_ge(hist_done, NP * b)
                for cc in range(2):
                    ch = 2 * p + cc
                    dve.wait_ge(sig_done, KD * b + ch + 1)
                    dve.wait_ge(a_full, KD * b + ch + 1)
                    dve.scalar_tensor_tensor(out=u[:, ch, HIST:], in0=ps_a[cc][:], scalar=vec[:, V_B1 + ch:V_B1 + ch + 1],
                                             in1=sig[:, cc, :], op0=ALU.add, op1=ALU.mult).then_inc(glu_done, 1)

            def taps(dve, b, p, j0, j1):
                for j in range(j0, j1):
                    for cc in range(2):
                        ch = 2 * p + cc
                        n = 2 * CW * (NP * b + p) + 2 * j + cc
                        if j == 0:
                            dve.wait_ge(glu_done, KD * b + ch + 1)
                            dve.tensor_scalar(v[:, ch, :], u[:, ch, 0:TB], wdw[:, ch, 0:1], vec[:, V_BDW + ch:V_BDW + ch + 1],
                                              ALU.mult, ALU.add).then_inc(tap_done, 1)
                        else:
                            dve.wait_ge(tap_done, n - 1)
                            dve.scalar_tensor_tensor(out=v[:, ch, :], in0=u[:, ch, j:j + TB], scalar=wdw[:, ch, j:j + 1],
                                                     in1=v[:, ch, :], op0=ALU.mult, op1=ALU.add).then_inc(tap_done, 1)
                if j1 == CW:
                    dve.wait_ge(tap_done, 2 * CW * (NP * b + p + 1))
                    chs = slice(2 * p, 2 * p + 2)
                    dve.tensor_copy(u[:, chs, 0:HIST], u[:, chs, TB:TB + HIST]).then_inc(hist_done, 1)

            def layer_norm1(dve, q):
                dve.wait_ge(mean_full, q + 1)
                dve.wait_ge(y_full, 2 * TT * q)
                for k in range(KD):
                    dve.tensor_tensor(s[:, k, :], v[:, k, :], ps_m[:], ALU.subtract).then_inc(ln1_done, 1)

            def layer_norm2(dve, q):
                dve.wait_ge(std_done, q + 1)
                dve.reciprocal(rstd[:], rstd[:]).then_inc(rstd_done, 1)
                dve.wait_ge(rstd_done, q + 1)
                for k in range(KD):
                    dve.tensor_tensor(s[:, k, :], s[:, k, :], rstd[:], ALU.mult).then_inc(ln2_done, 1)

            def residual(dve, q, i):
                dve.wait_ge(y_free, 2 * TT * q + 2 * i + 2)
                dve.wait_ge(xr_in[i % 2], 16 * (2 * q + i // 2 + 1))
                dve.tensor_tensor(ybuf[:, i, :], ybuf[:, i, :], xr[:, i % 2, :], ALU.add).then_inc(x1_done, 1)

            def second_norm(dve, q, i):
                dve.wait_ge(rstd2_done, 2 * q + i // 2 + 1)
                dve.wait_ge(h2_out[i % 2], 16 * (2 * q + i // 2))
                if i >= 2:
                    dve.wait_ge(t_full[1], before_router(q)[1] + i - 1)
                elif q:
                    dve.wait_ge(t_full[1], before_router(q - 1)[1] + TT)
                dve.scalar_tensor_tensor(out=h2[:, i % 2, :], in0=ybuf[:, i, :], scalar=r2[:, i:i + 1], in1=G2_row[:],
                                         op0=ALU.mult, op1=ALU.mult).then_inc(h2_half, 1)
                dve.wait_ge(h2_half, TT * q + i + 1)
                dve.tensor_tensor(h2[:, i % 2, :], h2[:, i % 2, :], sh2_row[:], ALU.add).then_inc(h2_done, 1)

            def dve_block(dve, b, first=False, last=False):
                q = b - 1
                if not first:
                    layer_norm1(dve, q)
                    dve.wait_ge(ln1_done, KD * b)
                taps(dve, b, 0, 0, CW)
                if not first:
                    layer_norm2(dve, q)
                glu(dve, b, 1)
                taps(dve, b, 1, 0, CW)
                glu(dve, b, 2)
                taps(dve, b, 2, 0, CW)
                glu(dve, b, 3)
                if first:
                    taps(dve, b, 3, 0, CW)
                else:
                    residual(dve, q, 0)
                    residual(dve, q, 1)
                    taps(dve, b, 3, 0, 12)
                    second_norm(dve, q, 0)
                    second_norm(dve, q, 1)
                    taps(dve, b, 3, 12, 24)
                    residual(dve, q, 2)
                    residual(dve, q, 3)
                    taps(dve, b, 3, 24, CW)
                if not last:
                    glu(dve, b + 1, 0)
                if not first:
                    second_norm(dve, q, 2)
                    second_norm(dve, q, 3)

            @block.vector
            def _(dve):
                dve.memset(eps_col[:], EPS).then_inc(pro_a, 1)
                dve.wait_ge(pro_t, 1)
                dve.tensor_copy(vec[:], ps_t[0][:, 0:7 * KD]).then_inc(pro_v, 1)
                dve.wait_ge(pro_t, 2)
                dve.tensor_copy(wdw[:].rearrange("p k j -> p (k j)"), ps_t[1][:, 0:KD * CW]).then_inc(pro_v, 1)
                dve.wait_ge(pro_a, 2)
                dve.tensor_copy(csil_bc, csil[:].unsqueeze(2).to_broadcast([P, KD, P])).then_inc(pro_v, 1)
                for j in range(NPIECE):
                    dve.wait_ge(mods_full, j + 1)
                    dve.tensor_tensor(mod_rows[j // 2][:, (j % 2) * H:(j % 2 + 1) * H], ps_a[j % 2][:], bada[j % 2],
                                      ALU.add).then_inc(mods_row, 1)
                    if j == 3:
                        for n in range(4):
                            dve.wait_ge(pro_t, 3 + n)
                            dve.tensor_copy(cols[:, 4 * n:4 * n + 4],
                                            ps_g[0][:].rearrange("p (k m) -> p k m", k=4)[:, :, 0]).then_inc(pro_v, 1)
                        dve.wait_ge(pro_v, 7)
                        dve.scalar_tensor_tensor(out=cols[:, KD:], in0=cols[:, KD:], scalar=1.0, in1=vec[:, V_NG:V_NG + KD],
                                                 op0=ALU.add, op1=ALU.mult).then_inc(pro_v, 1)
                dve.wait_ge(mods_row, NPIECE)
                dve.wait_ge(vec_in, 160)
                dve.scalar_tensor_tensor(out=G2_row[:], in0=G2_row[:], scalar=1.0, in1=ng2_row, op0=ALU.add,
                                         op1=ALU.mult).then_inc(pro_v, 1)
                dve.tensor_tensor(gb_row[:], b2_row, g1_row, ALU.mult).then_inc(pro_v, 1)
                dve.wait_ge(w2_in, 16)
                for k in range(KD):
                    dve.tensor_tensor(w2[:, k, :], w2[:, k, :], g1_row, ALU.mult).then_inc(pro_v, 1)
                dve.wait_ge(pro_v, 10 + KD)
                dve.wait_ge(consts, 5)
                glu(dve, 0, 0)
                for b in range(NB):
                    dve_block(dve, b, first=b == 0, last=b == NB - 1)
                layer_norm1(dve, NB - 1)
                layer_norm2(dve, NB - 1)
                for i in range(TT):
                    residual(dve, NB - 1, i)
                for i in range(TT):
                    second_norm(dve, NB - 1, i)

        moe = ExitStack()
        with moe:
            def mb(name, shape, dt=F32):
                return sb(name, shape, dt, moe)

            def ms(name):
                return sem(name, moe)

            NE = NT * E
            wi = mb("wi", [P, KD, 2 * DE])
            wo = mb("wo", [P, KE, D])
            xg = mb("xg", [P, D])
            xT = mb("xT", [P, KD, P])
            gate = mb("gate", [P, DE])
            hid = mb("hid", [P, DE])
            hidT = mb("hidT", [P, KE, P])
            ysb = mb("ysb", [P, D])
            rb = mb("rb", [P, E])
            ones = mb("ones", [P, P])
            below = mb("below", [P, P])
            pri = mb("pri", [P, E])
            thr = mb("thr", [P, NT])
            iota_p = mb("iota_p", [P, P])
            iota_t = mb("iota_t", [P, MTP])
            tokid = mb("tokid", [P, NT])
            zeros16 = mb("zeros16", [P, P], F16)
            scores = mb("scores", [P, NT, E])
            biased = mb("biased", [P, NT, E])
            tmp = mb("tmp", [P, NT, E])
            tmp2 = mb("tmp2", [P, NT, E])
            e1 = mb("e1", [P, NT, E])
            e2 = mb("e2", [P, NT, E])
            both = mb("both", [P, NT, E])
            cnt = mb("cnt", [P, NT, E])
            off = mb("off", [P, NT, E])
            gs = mb("gs", [P, NT, NG])
            gsel = mb("gsel", [P, NT, NG])
            tg = mb("tg", [P, NT, NG])
            mx = mb("mx", [P, NT])
            wts = mb("wts", [P, NT, 2])
            wsum = mb("wsum", [P, NT])
            total = mb("total", [P, E])
            ntile = mb("ntile", [P, E])
            cum = mb("cum", [P, E])
            base = mb("base", [P, E])
            onesE = mb("onesE", [P, E])
            cmp_t = mb("cmp_t", [P, MTP, E])
            slot_f = mb("slot_f", [P, 2, NT])
            slot_i = mb("slot_i", [P, 2, NT], I32)
            slot_hi = mb("slot_hi", [P, 2, NT], I32)
            slot_lo = mb("slot_lo", [P, 2, NT], I32)
            hi_f = mb("hi_f", [P, 2, NT])
            lo_f = mb("lo_f", [P, 2, NT])
            texp = mb("texp", [P, MTP])
            texp_i = mb("texp_i", [P, MTP], I32)
            fresh_f = mb("fresh_f", [P, MTP])
            fresh_i = mb("fresh_i", [P, MTP], I32)
            tok_i = mb("tok_i", [P, MTP], I32)
            sel_row = mb("sel_row", [P, 2, P], F16)
            sel_tile = mb("sel_tile", [P, 2, MTP], F16)
            idx = mb("idx", [P, 1], I32)
            cidx = mb("cidx", [P, 2, 2, 1], I32)
            ya = mb("ya", [P, 2, D])
            yb = mb("yb", [P, 2, D])
            x1r = mb("x1r", [P, 2, D])
            wcol = mb("wcol", [P, 2, 2])

            ps_gate, ps_up, ps_t0, ps_t1, ps_h, ps_y0, ps_y1, ps_r = bank

            pool_pass = ms("pool_pass2")
            mconst, rb_in = ms("mconst"), ms("rb_in")
            sc_done, route, both_done, rank_full, sel_done, sel_used = ms("sc_done"), ms("route"), ms("both_done"), ms("rank_full"), ms("sel_done"), ms("sel_used")
            tok_full, lists = ms("tok_full"), ms("lists")
            idx_done, xg_in = ms("idx_done"), ms("xg_in")
            xp0_full, xp1_full, xp0_free, xp1_free = ms("xp0_full"), ms("xp1_full"), ms("xp0_free"), ms("xp1_free")
            wi_in = [ms(f"wi_in{k}") for k in range(KD)]
            wo_in = [ms(f"wo_in{k}") for k in range(KE)]
            g1_step, g2_step = ms("g1_step"), ms("g2_step")
            gate_done, hid_done, hp_full, hidT_done = ms("gate_done"), ms("hid_done"), ms("hp_full"), ms("hidT_done")
            y0_free, y1_free, y_out = ms("y0_free"), ms("y1_free"), ms("y_out")
            cidx_done, wcol_done = ms("cidx_done"), ms("wcol_done")
            ya_in = [ms(f"ya_in{i}") for i in range(2)]
            yb_in = [ms(f"yb_in{i}") for i in range(2)]
            x1_in = [ms(f"x1_in{i}") for i in range(2)]
            ya_w, comb1, comb2 = ms("ya_w"), ms("comb1"), ms("comb2")
            comb3 = [ms(f"comb3_{i}") for i in range(2)]
            out_done = [ms(f"out_done{i}") for i in range(2)]

            out_rows = out.rearrange("o s d -> (o s) d")
            block = moe.enter_context(nc.Block())

            def load_x1(sp, n):
                for j in range(2):
                    sp.wait_ge(out_done[j], 16 * n)
                    sp.dma_start(x1r[:, j, :], x1_dram[bass.ds((2 * n + j) * P, P), :]).then_inc(x1_in[j], 16)

            def expert_in(e, k):
                return moe_w_in[0, bass.ds(e, 1), k * P:(k + 1) * P, :].rearrange("o p n -> (o p) n")

            def expert_out(e, k):
                return moe_w_out[0, bass.ds(e, 1), k * P:(k + 1) * P, :].rearrange("o p n -> (o p) n")

            def load_expert(sp, t, what, always=False):
                e = sp.value_load(texp_i[0:1, bass.ds(t, 1)], min_val=0, max_val=E - 1)
                new = 1 if always else sp.value_load(fresh_i[0:1, bass.ds(t, 1)], min_val=0, max_val=1)
                cond = {} if always else {"cond": new}
                if what == "in":
                    for k in range(KD):
                        sp.wait_ge(g1_step, KD * (t - 1) + k + 1)
                        sp.dma_start(wi[:, k, :], expert_in(e, k), **cond).then_inc(wi_in[k], 16)
                else:
                    for k in range(KE):
                        if not always:
                            sp.wait_ge(g2_step, KE * (t - 1) + k + 1)
                        sp.dma_start(wo[:, k, :], expert_out(e, k), **cond).then_inc(wo_in[k], 16)

            @block.sync
            def _(sp):
                sp.dma_start(rb[:], router_bias.rearrange("(o e) -> o e", o=1).to_broadcast([P, E])).then_inc(rb_in, 16)
                sp.wait_ge(lists, 1)
                e0 = sp.value_load(texp_i[0:1, 0:1], min_val=0, max_val=E - 1)
                for k in range(KD):
                    sp.dma_start(wi[:, k, :], expert_in(e0, k)).then_inc(wi_in[k], 16)
                load_expert(sp, 1, what="in")
                load_expert(sp, 0, what="out", always=True)
                with sp.Fori(1, MT - 1) as t:
                    load_expert(sp, t + 1, what="in")
                    load_expert(sp, t, what="out")
                load_expert(sp, MT - 1, what="out")
                load_x1(sp, 0)
                with sp.Fori(1, NT // 2) as n:
                    load_x1(sp, n)
                for j in range(2):
                    sp.wait_ge(out_done[j], 16 * NT // 2)

            def gather_outputs(pool, n):
                for j in range(2):
                    pool.wait_ge(comb3[j], n)
                    pool.wait_ge(ya_in[j], 16 * n)
                    pool.wait_ge(yb_in[j], 16 * n)
                    pool.sem_inc(pool_pass, 1)
                    for w in range(2):
                        pool.tensor_copy(cidx[:, j, w, :], slot_i[:, w, bass.ds(2 * n + j, 1)]).then_inc(cidx_done, 1)
                    pool.wait_ge(cidx_done, 4 * n + 2 * j + 2)
                    pool.sem_inc(pool_pass, 1)
                    pool.indirect_dma_start(ya[:, j, :], None, y_dram[:, :], bass.IndirectOffsetOnAxis(ap=cidx[:, j, 0, :], axis=0)).then_inc(ya_in[j], 16)
                    pool.indirect_dma_start(yb[:, j, :], None, y_dram[:, :], bass.IndirectOffsetOnAxis(ap=cidx[:, j, 1, :], axis=0)).then_inc(yb_in[j], 16)

            def gather(pool, t, first=False):
                if not first:
                    pool.wait_ge(xg_in, 16 * t)
                pool.sem_inc(pool_pass, 1)
                pool.tensor_copy(idx[:], tok_i[:, bass.ds(t, 1)]).then_inc(idx_done, 1)
                if not first:
                    pool.wait_ge(xp1_full, t)
                pool.wait_ge(idx_done, t + 1)
                pool.sem_inc(pool_pass, 1)
                pool.indirect_dma_start(xg[:], None, h2_dram[:, :], bass.IndirectOffsetOnAxis(ap=idx[:], axis=0)).then_inc(xg_in, 16)

            @block.gpsimd
            def _(pool):
                pool.memset(ones[:], 1.0).then_inc(mconst, 1)
                pool.memset(zeros16[:], 0.0).then_inc(mconst, 1)
                pool.memset(onesE[:], 1.0).then_inc(mconst, 1)
                pool.iota(pri[:], [[-1, E]], base=E, channel_multiplier=0, allow_small_or_imprecise_dtypes=True).then_inc(mconst, 1)
                pool.iota(thr[:], [[P, NT]], base=0, channel_multiplier=0, allow_small_or_imprecise_dtypes=True).then_inc(mconst, 1)
                pool.iota(iota_p[:], [[1, P]], base=0, channel_multiplier=0, allow_small_or_imprecise_dtypes=True).then_inc(mconst, 1)
                pool.iota(iota_t[:], [[1, MTP]], base=0, channel_multiplier=0, allow_small_or_imprecise_dtypes=True).then_inc(mconst, 1)
                pool.iota(tokid[:], [[P, NT]], base=0, channel_multiplier=1, allow_small_or_imprecise_dtypes=True).then_inc(mconst, 1)
                pool.wait_ge(mconst, 1)
                pool.affine_select(out=below[:], in_=ones[:], compare_op=ALU.is_gt, fill=0.0, base=0,
                                   pattern=[[1, P]], channel_multiplier=-1).then_inc(mconst, 1)
                pool.wait_ge(lists, 1)
                gather(pool, 0, first=True)
                with pool.Fori(1, MT) as t:
                    gather(pool, t)
                pool.wait_ge(y_out, 16 * MT)
                gather_outputs(pool, 0)
                with pool.Fori(1, NT // 2) as n:
                    gather_outputs(pool, n)

            def transpose_rows(pe, t, first=False):
                pe.wait_ge(xg_in, 16 * (t + 1))
                for ps, free, full, k0 in ((ps_t0, xp0_free, xp0_full, 0), (ps_t1, xp1_free, xp1_full, 4)):
                    if not first:
                        pe.wait_ge(free, t)
                    for k in range(4):
                        at = (k0 + k) * P
                        last = pe.transpose(ps[:, k * P:(k + 1) * P], xg[:, at:at + P], ident[:])
                    last.then_inc(full, 1)

            def ffn_in(pe, t, first=False):
                pe.wait_ge(xp0_free, t + 1)
                pe.wait_ge(xp1_free, t + 1)
                if not first:
                    pe.wait_ge(hid_done, t)
                for k in range(KD):
                    pe.wait_ge(wi_in[k], 16 * (t + 1))
                    pe.matmul(ps_gate[:], xT[:, k, :], wi[:, k, 0:DE], start=(k == 0), stop=(k == KD - 1))
                    pe.matmul(ps_up[:], xT[:, k, :], wi[:, k, DE:2 * DE], start=(k == 0), stop=(k == KD - 1)).then_inc(g1_step, 1)

            def transpose_hidden(pe, t):
                pe.wait_ge(hid_done, t + 1)
                pe.wait_ge(hidT_done, t)
                for k in range(KE):
                    last = pe.transpose(ps_h[:, k * P:(k + 1) * P], hid[:, k * P:(k + 1) * P], ident[:])
                last.then_inc(hp_full, 1)

            def ffn_out(pe, t):
                pe.wait_ge(hidT_done, t + 1)
                pe.wait_ge(y0_free, t)
                pe.wait_ge(y1_free, t)
                for k in range(KE):
                    pe.wait_ge(wo_in[k], 16 * (t + 1))
                    pe.matmul(ps_y0[:], hidT[:, k, :], wo[:, k, 0:H], start=(k == 0), stop=(k == KE - 1))
                    pe.matmul(ps_y1[:], hidT[:, k, :], wo[:, k, H:D], start=(k == 0), stop=(k == KE - 1)).then_inc(g2_step, 1)

            def pe_step(pe, t):
                ffn_in(pe, t + 1)
                transpose_hidden(pe, t)
                transpose_rows(pe, t + 2)
                ffn_out(pe, t)

            @block.tensor
            def _(pe):
                pe.wait_ge(mconst, 9)
                pe.wait_ge(both_done, 1)
                flat = both[:].rearrange("p t e -> p (t e)")
                pe.matmul(ps_t0[:, 0:NE], below[:], flat, start=True, stop=True)
                pe.matmul(ps_t1[:, 0:NE], ones[:], flat, start=True, stop=True).then_inc(rank_full, 1)
                pe.matmul(ps_r[:, 0:MTP], zeros16[:], zeros16[:, 0:MTP], start=True, stop=False, skip_group_check=True)
                with pe.Fori(0, NT) as i:
                    for w in range(2):
                        pe.wait_ge(sel_done, 4 * i + 2 * w + 2)
                        pe.matmul(ps_r[:, 0:MTP], sel_row[:, w, :], sel_tile[:, w, :], start=False, stop=False,
                                  skip_group_check=True).then_inc(sel_used, 1)
                pe.matmul(ps_r[:, 0:MTP], zeros16[:], zeros16[:, 0:MTP], start=False, stop=True,
                          skip_group_check=True).then_inc(tok_full, 1)
                transpose_rows(pe, 0, first=True)
                ffn_in(pe, 0, first=True)
                transpose_rows(pe, 1)
                pe_step(pe, 0)
                with pe.Fori(1, MT - 2) as t:
                    pe_step(pe, t)
                ffn_in(pe, MT - 1)
                for t in (MT - 2, MT - 1):
                    transpose_hidden(pe, t)
                    ffn_out(pe, t)

            def copy_rows(act, t):
                act.wait_ge(xp0_full, t + 1)
                act.copy(xT[:, 0:4, :].rearrange("p k m -> p (k m)"), ps_t0[:]).then_inc(xp0_free, 1)

            def act_gate(act, t):
                act.wait_ge(g1_step, KD * (t + 1))
                act.wait_ge(hid_done, t)
                act.activation(gate[:], ps_gate[:], ACT.Silu).then_inc(gate_done, 1)

            def copy_hidden(act, t):
                act.wait_ge(hp_full, t + 1)
                act.copy(hidT[:].rearrange("p k m -> p (k m)"), ps_h[:]).then_inc(hidT_done, 1)

            def copy_out(act, t):
                act.wait_ge(g2_step, KE * (t + 1))
                act.wait_ge(y_out, 16 * t)
                act.copy(ysb[:, 0:H], ps_y0[:]).then_inc(y0_free, 1)
                act.wait_ge(y0_free, t + 1)
                act.wait_ge(y1_free, t + 1)
                act.dma_start(y_dram[bass.ds(t * P, P), :], ysb[:]).then_inc(y_out, 16)

            def act_step(act, t):
                act_gate(act, t + 1)
                copy_hidden(act, t)
                copy_rows(act, t + 2)
                copy_out(act, t)

            def weigh(act, n):
                for j in range(2):
                    act.wait_ge(ya_in[j], 16 * (n + 1))
                    act.wait_ge(wcol_done, 2 * n + j + 1)
                    act.activation(ya[:, j, :], ya[:, j, :], ACT.Copy, scale=wcol[:, j, 0:1]).then_inc(ya_w, 1)
                for j in range(2):
                    act.wait_ge(comb3[j], n + 1)
                    act.dma_start(out_rows[bass.ds((2 * n + j) * P, P), :], x1r[:, j, :]).then_inc(out_done[j], 16)

            @block.scalar
            def _(act):
                act.activation(scores[:], logits[:], ACT.Sigmoid).then_inc(sc_done, 1)
                copy_rows(act, 0)
                act_gate(act, 0)
                copy_rows(act, 1)
                act_step(act, 0)
                with act.Fori(1, MT - 2) as t:
                    act_step(act, t)
                act_gate(act, MT - 1)
                for t in (MT - 2, MT - 1):
                    copy_hidden(act, t)
                    copy_out(act, t)
                weigh(act, 0)
                with act.Fori(1, NT // 2) as n:
                    weigh(act, n)

            def dve_step(dve, t):
                dve_hidden(dve, t + 1)
                dve_rows(dve, t + 2)
                dve_out(dve, t)

            def combine(dve, n):
                for j in range(2):
                    dve.wait_ge(comb1, 2 * n)
                    dve.wait_ge(ya_w, 2 * n)
                    dve.tensor_copy(wcol[:, j, :], wts[:, bass.ds(2 * n + j, 1), :].rearrange("p o w -> p (o w)")).then_inc(wcol_done, 1)
                for j in range(2):
                    dve.wait_ge(ya_w, 2 * n + j + 1)
                    dve.wait_ge(yb_in[j], 16 * (n + 1))
                    dve.wait_ge(wcol_done, 2 * n + j + 1)
                    dve.scalar_tensor_tensor(out=ya[:, j, :], in0=yb[:, j, :], scalar=wcol[:, j, 1:2], in1=ya[:, j, :],
                                             op0=ALU.mult, op1=ALU.add).then_inc(comb1, 1)
                for j in range(2):
                    dve.wait_ge(comb1, 2 * n + j + 1)
                    dve.tensor_tensor(ya[:, j, :], ya[:, j, :], g2_row[:], ALU.mult).then_inc(comb2, 1)
                for j in range(2):
                    dve.wait_ge(comb2, 2 * n + j + 1)
                    dve.wait_ge(x1_in[j], 16 * (n + 1))
                    dve.tensor_tensor(x1r[:, j, :], ya[:, j, :], x1r[:, j, :], ALU.add).then_inc(comb3[j], 1)

            def one_hots(dve, i):
                for w in range(2):
                    dve.wait_ge(sel_used, 2 * i)
                    dve.tensor_scalar(sel_row[:, w, :], iota_p[:], lo_f[:, w, bass.ds(i, 1)], None, ALU.is_equal).then_inc(sel_done, 1)
                    dve.tensor_scalar(sel_tile[:, w, :], iota_t[:], hi_f[:, w, bass.ds(i, 1)], tokid[:, bass.ds(i, 1)],
                                      ALU.is_equal, ALU.mult).then_inc(sel_done, 1)

            def dve_rows(dve, t):
                dve.wait_ge(xp1_full, t + 1)
                dve.tensor_copy(xT[:, 4:8, :].rearrange("p k m -> p (k m)"), ps_t1[:]).then_inc(xp1_free, 1)

            def dve_hidden(dve, t):
                dve.wait_ge(gate_done, t + 1)
                dve.wait_ge(g1_step, KD * (t + 1))
                dve.wait_ge(hp_full, t)
                dve.tensor_tensor(hid[:], gate[:], ps_up[:], ALU.mult).then_inc(hid_done, 1)

            def dve_out(dve, t):
                dve.wait_ge(g2_step, KE * (t + 1))
                dve.wait_ge(y_out, 16 * t)
                dve.tensor_copy(ysb[:, H:D], ps_y1[:]).then_inc(y1_free, 1)

            @block.vector
            def _(dve):
                steps = [0]

                def then(ins):
                    steps[0] += 1
                    ins.then_inc(route, 1)
                    dve.wait_ge(route, steps[0])

                def bc_e(ap):
                    return ap.unsqueeze(2).to_broadcast([P, NT, E])

                def first_max(dst, src, t, n):
                    then(dve.tensor_reduce(mx[:], src, AX_X, ALU.max))
                    wide = mx[:].unsqueeze(2).to_broadcast([P, NT, n])
                    then(dve.tensor_tensor(t, src, wide, ALU.is_equal))
                    then(dve.tensor_tensor(t, t, pri[:, 0:n].unsqueeze(1).to_broadcast([P, NT, n]), ALU.mult))
                    then(dve.tensor_reduce(mx[:], t, AX_X, ALU.max))
                    then(dve.tensor_tensor(dst, t, wide, ALU.is_equal))

                dve.wait_ge(mconst, 9)
                dve.wait_ge(rb_in, 16)
                dve.wait_ge(sc_done, 1)
                then(dve.tensor_tensor(biased[:], scores[:], rb[:].unsqueeze(1).to_broadcast([P, NT, E]), ALU.add))
                bv = biased[:].rearrange("p t (g j) -> p (t g) j", j=EG)
                gflat, tflat = gs[:].rearrange("p t g -> p (t g)"), tg[:].rearrange("p t g -> p (t g)")
                pairs = [(i, j) for i in range(EG) for j in range(i + 1, EG)]
                for n, (i, j) in enumerate(pairs):
                    then(dve.tensor_tensor(gflat if n == 0 else tflat, bv[:, :, i], bv[:, :, j], ALU.add))
                    if n:
                        then(dve.tensor_tensor(gflat, gflat, tflat, ALU.max))
                first_max(gsel[:], gs[:], tg[:], NG)
                then(dve.tensor_scalar(tg[:], gsel[:], -1.0, BIG, ALU.add, ALU.mult))
                for j in range(EG):
                    view = biased[:].rearrange("p t (g j) -> p t g j", j=EG)[:, :, :, j]
                    then(dve.tensor_tensor(tmp2[:].rearrange("p t (g j) -> p t g j", j=EG)[:, :, :, j], view, tg[:], ALU.add))
                first_max(e1[:], tmp2[:], tmp[:], E)
                then(dve.scalar_tensor_tensor(out=tmp2[:].rearrange("p t e -> p (t e)"), in0=e1[:].rearrange("p t e -> p (t e)"),
                                              scalar=-3.0 * BIG, in1=tmp2[:].rearrange("p t e -> p (t e)"), op0=ALU.mult, op1=ALU.add))
                first_max(e2[:], tmp2[:], tmp[:], E)
                dve.tensor_tensor(both[:], e1[:], e2[:], ALU.add).then_inc(both_done, 1)
                for w, e in enumerate((e1, e2)):
                    then(dve.tensor_tensor(tmp[:], e[:], scores[:], ALU.mult))
                    then(dve.tensor_reduce(wts[:, :, w], tmp[:], AX_X, ALU.add))
                then(dve.tensor_tensor(wsum[:], wts[:, :, 0], wts[:, :, 1], ALU.add))
                then(dve.reciprocal(wsum[:], wsum[:]))
                then(dve.tensor_tensor(wts[:], wts[:], wsum[:].unsqueeze(2).to_broadcast([P, NT, 2]), ALU.mult))
                dve.wait_ge(rank_full, 1)
                then(dve.tensor_copy(cnt[:].rearrange("p t e -> p (t e)"), ps_t1[:, 0:NE]))
                then(dve.memset(off[:, 0, :], 0.0))
                for t in range(1, NT):
                    then(dve.tensor_tensor(off[:, t, :], off[:, t - 1, :], cnt[:, t - 1, :], ALU.add))
                then(dve.tensor_tensor(total[:], off[:, NT - 1, :], cnt[:, NT - 1, :], ALU.add))
                ct = cmp_t[:, 0:E, :].rearrange("p e k -> p e k")
                then(dve.tensor_tensor(ct[:, :, 0:NT], total[:].unsqueeze(2).to_broadcast([P, E, NT]),
                                       thr[:].unsqueeze(1).to_broadcast([P, E, NT]), ALU.is_gt))
                then(dve.tensor_reduce(ntile[:], ct[:, :, 0:NT], AX_X, ALU.add))
                then(dve.tensor_tensor_scan(cum[:], onesE[:], ntile[:], 0.0, ALU.mult, ALU.add))
                then(dve.tensor_tensor(base[:], cum[:], ntile[:], ALU.subtract))
                then(dve.tensor_scalar(base[:], base[:], float(P), None, ALU.mult))
                then(dve.tensor_tensor(cmp_t[:], cum[:].unsqueeze(1).to_broadcast([P, MTP, E]),
                                       iota_t[:].unsqueeze(2).to_broadcast([P, MTP, E]), ALU.is_le))
                then(dve.tensor_reduce(texp[:], cmp_t[:], AX_X, ALU.add))
                then(dve.tensor_scalar(texp[:], texp[:], float(E - 1), None, ALU.min))
                then(dve.tensor_copy(texp_i[:], texp[:]))
                then(dve.memset(fresh_f[:], 1.0))
                then(dve.tensor_tensor(fresh_f[:, 1:MTP], texp[:, 1:MTP], texp[:, 0:MT], ALU.not_equal))
                then(dve.tensor_copy(fresh_i[:], fresh_f[:]))
                then(dve.tensor_tensor(off[:].rearrange("p t e -> p (t e)"), off[:].rearrange("p t e -> p (t e)"), ps_t0[:, 0:NE], ALU.add))
                then(dve.tensor_tensor(off[:], off[:], base[:].unsqueeze(1).to_broadcast([P, NT, E]), ALU.add))
                for w, e in enumerate((e1, e2)):
                    then(dve.tensor_tensor(tmp[:], e[:], off[:], ALU.mult))
                    then(dve.tensor_reduce(slot_f[:, w, :], tmp[:], AX_X, ALU.add))
                then(dve.tensor_copy(slot_i[:], slot_f[:]))
                then(dve.tensor_scalar(slot_hi[:], slot_i[:], 7, None, ALU.arith_shift_right))
                then(dve.tensor_scalar(slot_lo[:], slot_i[:], P - 1, None, ALU.bitwise_and))
                then(dve.tensor_copy(hi_f[:], slot_hi[:]))
                then(dve.tensor_copy(lo_f[:], slot_lo[:]))
                one_hots(dve, 0)
                with dve.Fori(1, NT) as i:
                    one_hots(dve, i)
                dve.wait_ge(tok_full, 1)
                dve.tensor_copy(tok_i[:], ps_r[:, 0:MTP]).then_inc(lists, 1)
                dve_rows(dve, 0)
                dve_hidden(dve, 0)
                dve_rows(dve, 1)
                dve_step(dve, 0)
                with dve.Fori(1, MT - 2) as t:
                    dve_step(dve, t)
                dve_hidden(dve, MT - 1)
                for t in (MT - 2, MT - 1):
                    dve_out(dve, t)
                combine(dve, 0)
                with dve.Fori(1, NT // 2) as n:
                    combine(dve, n)

_INS = ['x', 'c', 'norm_mix_g', 'norm_ffn_g', 'w_ada', 'b_ada', 'conv_w_pw1', 'conv_b_pw1', 'conv_w_dw', 'conv_b_dw',
        'conv_ln_g', 'conv_ln_b', 'conv_w_pw2', 'conv_b_pw2', 'router_w', 'router_bias', 'moe_w_in', 'moe_w_out']


def kernel(**inputs):
    import numpy as _np
    import concourse.bacc as _bacc
    from concourse import mybir as _mybir
    from concourse.bass_utils import run_bass_kernel_spmd as _run

    nc = _bacc.Bacc("TRN2", target_bir_lowering=False, num_devices=1)
    arrays, args = {}, []
    for name in _INS:
        a = _np.ascontiguousarray(inputs[name])
        arrays[f"in_{name}_dram"] = a
        args.append(nc.dram_tensor(f"in_{name}_dram", a.shape, _mybir.dt.from_np(a.dtype), kind="ExternalInput").ap())
    shape = tuple(inputs["x"].shape)
    out = nc.dram_tensor("out_0_dram", shape, _mybir.dt.float32, kind="ExternalOutput").ap()
    kernel_program(nc, *args, out)
    r = _run(nc, [arrays], core_ids=[0])
    return r.results[0]["out_0_dram"]
```

```python
from contextlib import ExitStack

import concourse.bass as bass
from concourse import mybir

F32 = mybir.dt.float32
F32R = mybir.dt.float32r
F16 = mybir.dt.float16
BF16 = mybir.dt.bfloat16
I32 = mybir.dt.int32
ALU = mybir.AluOpType
ACT = mybir.ActivationFunctionType
AX_X = mybir.AxisListType.X

P = 128
EPS = 1e-6
BIG = 1e30


def kernel_program(nc, x, c, norm_mix_g, norm_ffn_g, w_ada, b_ada, conv_w_pw1, conv_b_pw1, conv_w_dw,
                   conv_b_dw, conv_ln_g, conv_ln_b, conv_w_pw2, conv_b_pw2, router_w, router_bias,
                   moe_w_in, moe_w_out, out):
    _, S, D = x.shape
    KD = D // P
    TB = 512
    NB = S // TB
    TT = TB // P
    NT = S // P
    CW = conv_w_dw.shape[1]
    HIST = CW - 1
    NP = KD // 2
    E = router_w.shape[1]
    NG = 4
    EG = E // NG
    DE = moe_w_out.shape[2]
    KE = DE // P
    MT = 2 * S // P + E - 1
    MTP = MT + 1
    H = D // 2
    LO = 32
    NR = 4
    NPIECE = w_ada.shape[2] // H

    x1_dram = nc.dram_tensor("x1_scratch", (S, D), F32, kind="Internal").ap()
    h2_dram = nc.dram_tensor("h2_scratch", (S, D), F32, kind="Internal").ap()
    y_dram = nc.dram_tensor("y_scratch", (MT * P, D), F32, kind="Internal").ap()

    keep = ExitStack()
    with keep:
        def sem(name, ctx=keep):
            return ctx.enter_context(nc.semaphore(name))

        def sb(name, shape, dt=F32, ctx=keep):
            return ctx.enter_context(nc.sbuf_tensor(name, shape, dt))

        ident = sb("ident", [P, P])
        g2_row = sb("g2_row", [P, D])
        logits = sb("logits", [P, NT, E])
        bank = [keep.enter_context(nc.psum_tensor(f"bank{i}", [P, 512], F32)) for i in range(8)]

        conv = ExitStack()
        with conv:
            def cb(name, shape, dt=F32):
                return sb(name, shape, dt, conv)

            def cs(name):
                return sem(name, conv)

            ps_a, ps_g = [bank[0], bank[1]], [bank[2], bank[3]]
            ps_m, ps_y, ps_t = bank[4], bank[5], [bank[6], bank[7]]

            w1 = cb("w1", [P, 2, KD, 2, P])
            w2 = cb("w2", [P, KD, D])
            xt = cb("xt", [P, TT, D])
            hT = cb("hT", [P, KD, TB])
            u = cb("u", [P, KD, HIST + TB])
            v = cb("v", [P, KD, TB])
            s = cb("s", [P, KD, TB])
            ybuf = cb("ybuf", [P, TT, D])
            xr = cb("xr", [P, 2, D])
            h2 = cb("h2", [P, 2, D])
            h2T = cb("h2T", [P, KD, P])
            sig = cb("sig", [P, 2, TB])
            sq = cb("sq", [P, 2, TB])
            rstd = cb("rstd", [P, TB])
            eps_col = cb("eps_col", [P, 1])
            junk = cb("junk", [P, 2, D], BF16)
            gb_row = cb("gb_row", [P, D], F32R)
            G2_row = cb("G2_row", [P, D])
            sh2_row = cb("sh2_row", [P, D])
            ones_mean = cb("ones_mean", [P, P])
            ones_hl = cb("ones_hl", [LO + 1, P], F32R)
            chsum = cb("chsum", [P, TB])
            vec_rows = cb("vec_rows", [7 * KD, P])
            vec = cb("vec", [P, 7 * KD])
            wdw_rows = cb("wdw_rows", [CW, D])
            wdw = cb("wdw", [P, KD, CW])
            csil = cb("csil", [P, KD])
            cols = cb("cols", [P, 2 * KD])
            rw = cb("rw", [P, KD, E])
            small = cb("small", [P, 8, TT])
            half = cb("half", [P, TT])

            V_NG, V_B1, V_BDW, V_LG, V_LB, V_C = 0, KD, 3 * KD, 4 * KD, 5 * KD, 6 * KD
            ada = [v, s]
            hl_f32 = chsum[0:LO + 1, 0:P]
            csil_bc = xr[:, 0, :].rearrange("p (k m) -> p k m", k=KD)
            bada = [h2[:, 1, i * H:(i + 1) * H] for i in range(2)]
            sh1_row, sc1_row = ybuf[:, 0, :], ybuf[:, 1, :]
            g1_row = ybuf[:, 2, :]
            b2_row, ng2_row = ybuf[:, 3, :], h2[:, 0, :]
            mod_rows = [sh1_row, sc1_row, g1_row, sh2_row[:], G2_row[:], g2_row[:]]
            ss1, r1, ss2, r2 = (small[:, i, :] for i in range(4))
            m1, m2 = small[:, 4, :], small[:, 5, :]

            consts = cs("consts")
            ident0 = cs("ident0")
            vec_in = cs("vec_in")
            w2_in = cs("w2_in")
            ada_in = [cs(f"ada_in{i}") for i in range(2)]
            pro_t = cs("pro_t")
            pro_v = cs("pro_v")
            pro_a = cs("pro_a")
            mods_full = cs("mods_full")
            mods_row = cs("mods_row")
            x_in = [cs(f"x_in{i}") for i in range(TT)]
            w1_in = [cs(f"w1_in{i}") for i in range(2)]
            xr_in = [cs(f"xr_in{i}") for i in range(2)]
            ss1_done, rstd1_done, xn_done = cs("ss1_done"), cs("rstd1_done"), cs("xn_done")
            ms1_done, ms2_done = cs("ms1_done"), cs("ms2_done")
            t_full = [cs(f"t_full{i}") for i in range(2)]
            t_free = [cs(f"t_free{i}") for i in range(2)]
            g_full, a_full = cs("g_full"), cs("a_full")
            sig_done, glu_done = cs("sig_done"), cs("glu_done")
            tap_done, hist_done = cs("tap_done"), cs("hist_done")
            mean_full, ln1_done = cs("mean_full"), cs("ln1_done")
            sq_done, var_full = cs("sq_done"), cs("var_full")
            vsum_step, sqsum_step = cs("vsum_step"), cs("sqsum_step")
            NSUM = KD - 1
            std_done, rstd_done, ln2_done, silu_done = cs("std_done"), cs("rstd_done"), cs("ln2_done"), cs("silu_done")
            y_full, y_free = cs("y_full"), cs("y_free")
            x1_done, ss2_done, rstd2_done = cs("x1_done"), cs("ss2_done"), cs("rstd2_done")
            h2_half, h2_done = cs("h2_half"), cs("h2_done")
            x1_out = [cs(f"x1_out{i}") for i in range(TT)]
            h2_out = [cs(f"h2_out{i}") for i in range(2)]

            def before_x(b):
                tiles = TT * max(0, b - 2)
                return TT * b + 2 * tiles, TT * b + tiles

            def before_router(q, i):
                xs = TT * min(NB, q + 3)
                return xs + 2 * (TT * q + i), xs + TT * q + i

            def tile_rows(ap, b, i):
                return ap[b * TB + i * P:b * TB + (i + 1) * P, :]

            x_rows = x.rearrange("o s d -> (o s) d")

            block = conv.enter_context(nc.Block())

            def load_x(sp, b):
                for i in range(TT):
                    sp.dma_start(xt[:, i, :], tile_rows(x_rows, b, i)).then_inc(x_in[i], 16)

            def load_w1(sp, b, p):
                for cc in range(2):
                    if b or p:
                        sp.wait_ge(a_full, KD * b + 2 * p + cc - 1)
                    ch = 2 * p + cc
                    for ag in range(2):
                        col = ag * D + ch * P
                        sp.dma_start(w1[:, cc, :, ag, :], conv_w_pw1[0, :, col:col + P].rearrange(
                            "(k p) m -> p k m", p=P)).then_inc(w1_in[cc], 16)

            def load_xr(sp, q, tiles):
                for i in tiles:
                    if i >= 2:
                        sp.wait_ge(x1_done, TT * q + i - 1)
                    else:
                        sp.wait_ge(x1_done, TT * q)
                    sp.dma_start(xr[:, i % 2, :], tile_rows(x_rows, q, i)).then_inc(xr_in[i % 2], 16)

            def sp_block(sp, b, first=False, last=False):
                for p in range(1, NP):
                    load_w1(sp, b, p)
                    if p == 1 and not last:
                        sp.wait_ge(t_full[1], before_x(b)[1] + 4)
                        load_x(sp, b + 1)
                    if p == 2 and not first:
                        load_xr(sp, b - 1, (0, 1))
                if not last:
                    load_w1(sp, b + 1, 0)
                if not first:
                    load_xr(sp, b - 1, (2, 3))

            @block.sync
            def _(sp):
                vecs = [(norm_mix_g, V_NG, KD), (conv_b_pw1, V_B1, 2 * KD), (conv_b_dw, V_BDW, KD),
                        (conv_ln_g, V_LG, KD), (conv_ln_b, V_LB, KD), (c, V_C, KD)]
                for t, at, n in vecs:
                    sp.dma_start(vec_rows[at:at + n, :], t.rearrange("o (k p) -> (o k) p", p=P)).then_inc(vec_in, 16)
                sp.dma_start(wdw_rows[:], conv_w_dw[0]).then_inc(vec_in, 16)
                sp.dma_start(rw[:], router_w.rearrange("(k p) e -> p k e", p=P)).then_inc(vec_in, 16)
                sp.dma_start(b2_row, conv_b_pw2.to_broadcast([P, D])).then_inc(vec_in, 16)
                sp.dma_start(ng2_row, norm_ffn_g.to_broadcast([P, D])).then_inc(vec_in, 16)
                for j in range(NPIECE):
                    if j >= 2:
                        sp.wait_ge(mods_row, j - 1)
                    sp.dma_start(ada[j % 2][:], w_ada[0].rearrange("(k p) n -> p k n", p=P)[:, :, j * H:(j + 1) * H]).then_inc(ada_in[j % 2], 16)
                    sp.dma_start(bada[j % 2], b_ada[:, j * H:(j + 1) * H].to_broadcast([P, H])).then_inc(ada_in[j % 2], 16)
                    if j == 1:
                        load_x(sp, 0)
                sp.dma_start(w2[:], conv_w_pw2[0].rearrange("(k p) n -> p k n", p=P)).then_inc(w2_in, 16)
                load_w1(sp, 0, 0)
                for b in range(NB):
                    sp_block(sp, b, first=b == 0, last=b == NB - 1)
                load_xr(sp, NB - 1, range(TT))
                for i in range(TT):
                    sp.wait_ge(x1_out[i], 16 * NB)
                for i in range(2):
                    sp.wait_ge(h2_out[i], 16 * NB * TT // 2)

            def rstd_of_x(pool, b):
                pool.wait_ge(ss1_done, TT * (b + 1))
                pool.tensor_scalar(m1, ss1, 1.0 / D, EPS, ALU.mult, ALU.add).then_inc(ms1_done, 1)
                pool.wait_ge(ms1_done, b + 1)
                pool.wait_ge(xn_done, TT * b)
                pool.tensor_tensor(r1, m1, half[:], ALU.pow).then_inc(rstd1_done, 1)

            def sum_v(pool, b, p):
                pool.wait_ge(tap_done, 2 * CW * (NP * b + p + 1))
                if p == 0:
                    if b == 0:
                        pool.wait_ge(pro_v, 13 + KD)
                    pool.wait_ge(var_full, b)
                    pool.tensor_tensor(chsum[:], v[:, 0, :], v[:, 1, :], ALU.add).then_inc(vsum_step, 1)
                else:
                    for ch in (2 * p, 2 * p + 1):
                        pool.wait_ge(vsum_step, NSUM * b + ch - 1)
                        pool.tensor_tensor(chsum[:], chsum[:], v[:, ch, :], ALU.add).then_inc(vsum_step, 1)

            def sum_squares(pool, q):
                pool.wait_ge(mean_full, q + 1)
                for k in range(1, KD):
                    pool.wait_ge(sq_done, KD * q + k + 1)
                    if k > 1:
                        pool.wait_ge(sqsum_step, NSUM * q + k - 1)
                    pool.tensor_tensor(chsum[:], sq[:, 0, :] if k == 1 else chsum[:], sq[:, k % 2, :],
                                       ALU.add).then_inc(sqsum_step, 1)

            def store_x1(pool, q, j):
                for i in (2 * j, 2 * j + 1):
                    pool.wait_ge(x1_done, TT * q + i + 1)
                    pool.dma_start(tile_rows(x1_dram, q, i), ybuf[:, i, :]).then_inc(x1_out[i], 16)
                pool.wait_ge(ss2_done, TT * q + 2 * j + 2)
                pair = slice(2 * j, 2 * j + 2)
                pool.tensor_scalar(m2[:, pair], ss2[:, pair], 1.0 / D, EPS, ALU.mult, ALU.add).then_inc(ms2_done, 1)
                pool.wait_ge(ms2_done, 2 * q + j + 1)
                pool.wait_ge(h2_half, TT * q)
                pool.tensor_tensor(r2[:, pair], m2[:, pair], half[:, pair], ALU.pow).then_inc(rstd2_done, 1)

            def store_h2(pool, q, j):
                for i in (2 * j, 2 * j + 1):
                    pool.wait_ge(h2_done, TT * q + i + 1)
                    pool.dma_start(tile_rows(h2_dram, q, i), h2[:, i % 2, :]).then_inc(h2_out[i % 2], 16)

            def pool_block(pool, b, first=False, last=False):
                if not first:
                    sum_squares(pool, b - 1)
                sum_v(pool, b, 0)
                if not last:
                    rstd_of_x(pool, b + 1)
                sum_v(pool, b, 1)
                sum_v(pool, b, 2)
                if not first:
                    store_x1(pool, b - 1, 0)
                    store_h2(pool, b - 1, 0)
                    store_x1(pool, b - 1, 1)
                sum_v(pool, b, 3)
                if not first:
                    store_h2(pool, b - 1, 1)

            @block.gpsimd
            def _(pool):
                pool.memset(ident[:], 0.0).then_inc(ident0, 1)
                pool.wait_ge(ident0, 1)
                pool.affine_select(out=ident[:], in_=ident[:], compare_op=ALU.not_equal, fill=1.0, base=0,
                                   pattern=[[-1, P]], channel_multiplier=1).then_inc(consts, 1)
                pool.memset(ones_mean[:], 1.0 / D).then_inc(consts, 1)
                pool.memset(hl_f32, 0.0).then_inc(consts, 1)
                pool.memset(half[:], -0.5).then_inc(consts, 1)
                pool.memset(u[:, :, 0:HIST], 0.0).then_inc(consts, 1)
                pool.wait_ge(consts, 5)
                pool.memset(hl_f32[0:1, :], 1.0).then_inc(consts, 1)
                pool.memset(hl_f32[LO:LO + 1, :], 1.0).then_inc(consts, 1)
                pool.wait_ge(consts, 7)
                rstd_of_x(pool, 0)
                for b in range(NB):
                    pool_block(pool, b, first=b == 0, last=b == NB - 1)
                sum_squares(pool, NB - 1)
                for j in range(2):
                    store_x1(pool, NB - 1, j)
                    store_h2(pool, NB - 1, j)

            def transpose_x(pe, b):
                pe.wait_ge(xn_done, TT * (b + 1))
                for k in range(KD):
                    n = before_x(b)[k % 2] + k // 2
                    if n:
                        pe.wait_ge(t_free[k % 2], n)
                    for i in range(TT):
                        last = pe.transpose(ps_t[k % 2][:, i * P:(i + 1) * P], xt[:, i, k * P:(k + 1) * P], ident[:])
                    last.then_inc(t_full[k % 2], 1)

            def pointwise1(pe, b, p):
                if p == 0:
                    for t in range(2):
                        pe.wait_ge(t_free[t], before_x(b)[t] + 4)
                for cc in range(2):
                    pe.wait_ge(w1_in[cc], 32 * (NP * b + p + 1))
                    if b or p:
                        pe.wait_ge(glu_done, KD * b + 2 * p + cc - 1)
                    for ps, ag, full in ((ps_g, 1, g_full), (ps_a, 0, a_full)):
                        for k in range(KD):
                            last = pe.matmul(ps[cc][:], w1[:, cc, k, ag, :], hT[:, k, :], start=(k == 0), stop=(k == KD - 1))
                        last.then_inc(full, 1)

            def mean(pe, b):
                pe.wait_ge(vsum_step, NSUM * (b + 1))
                pe.wait_ge(std_done, b)
                pe.matmul(ps_m[:], ones_mean[:], chsum[:], start=True, stop=True).then_inc(mean_full, 1)

            def variance(pe, q):
                pe.wait_ge(ln1_done, KD * (q + 1))
                pe.wait_ge(sqsum_step, NSUM * (q + 1))
                pe.matmul(ps_m[:], ones_mean[:], chsum[:], start=True, stop=True).then_inc(var_full, 1)

            def pointwise2(pe, q, i):
                if i == 0:
                    pe.wait_ge(silu_done, KD * (q + 1))
                    pe.wait_ge(pro_v, 13 + KD)
                for h in range(2):
                    pe.wait_ge(y_free, 2 * TT * q + 2 * i + h)
                    cols_h = slice(h * H, (h + 1) * H)
                    for k in range(KD):
                        pe.matmul(ps_y[:], s[:, k, i * P:(i + 1) * P], w2[:, k, cols_h], start=(k == 0), stop=False)
                    pe.matmul(ps_y[:], ones_hl[:], gb_row[0:LO + 1, cols_h], start=False, stop=True).then_inc(y_full, 1)

            def router(pe, q, i):
                n0, n1 = before_router(q, i)
                pe.wait_ge(h2_done, TT * q + i + 1)
                for t, n in ((0, n0), (1, n1)):
                    pe.wait_ge(t_free[t], n)
                    for k in range(4):
                        at = (4 * t + k) * P
                        last = pe.transpose(ps_t[t][:, k * P:(k + 1) * P], h2[:, i % 2, at:at + P], ident[:])
                    last.then_inc(t_full[t], 1)
                pe.wait_ge(t_free[0], n0 + 1)
                pe.wait_ge(t_free[1], n1 + 1)
                for k in range(KD):
                    last = pe.matmul(ps_t[0][:, 0:E], h2T[:, k, :], rw[:, k, :], start=(k == 0), stop=(k == KD - 1))
                last.then_inc(t_full[0], 1)

            def pe_block(pe, b, first=False, last=False):
                q = b - 1
                pointwise1(pe, b, 1)
                if b >= 2:
                    router(pe, q - 1, 2)
                    router(pe, q - 1, 3)
                if not first:
                    variance(pe, q)
                pointwise1(pe, b, 2)
                if not first:
                    pointwise2(pe, q, 0)
                pointwise1(pe, b, 3)
                if not first:
                    pointwise2(pe, q, 1)
                    pointwise2(pe, q, 2)
                if not first:
                    pointwise2(pe, q, 3)
                if not last:
                    transpose_x(pe, b + 1)
                    pointwise1(pe, b + 1, 0)
                if not first:
                    router(pe, q, 0)
                    router(pe, q, 1)
                mean(pe, b)

            @block.tensor
            def _(pe):
                pe.wait_ge(consts, 3)
                pe.wait_ge(vec_in, 160)
                pe.transpose(ps_t[0][:, 0:7 * KD], vec_rows[:], ident[0:7 * KD, 0:7 * KD]).then_inc(pro_t, 1)
                for k in range(KD):
                    last = pe.transpose(ps_t[1][:, k * CW:(k + 1) * CW], wdw_rows[:, k * P:(k + 1) * P], ident[0:CW, 0:CW])
                last.then_inc(pro_t, 1)
                pe.wait_ge(pro_v, 3)
                for j in range(NPIECE):
                    pe.wait_ge(ada_in[j % 2], 32 * (j // 2 + 1))
                    if j >= 2:
                        pe.wait_ge(mods_row, j - 1)
                    for k in range(KD):
                        last = pe.matmul(ps_a[j % 2][:], csil_bc[:, k, :], ada[j % 2][:, k, :], start=(k == 0), stop=(k == KD - 1))
                    last.then_inc(mods_full, 1)
                    if j == 3:
                        pe.wait_ge(mods_row, 4)
                        for r, row in enumerate((sh1_row, sc1_row)):
                            for n in range(2):
                                if n or r:
                                    pe.wait_ge(pro_v, 3 + 2 * r + n)
                                for k in range(4):
                                    at = (4 * n + k) * P
                                    last = pe.transpose(ps_g[0][:, k * P:(k + 1) * P], row[:, at:at + P], ident[:])
                                last.then_inc(pro_t, 1)
                transpose_x(pe, 0)
                pe.wait_ge(mods_row, NPIECE)
                pe.wait_ge(pro_v, 7)
                pointwise1(pe, 0, 0)
                for b in range(NB):
                    pe_block(pe, b, first=b == 0, last=b == NB - 1)
                router(pe, NB - 2, 2)
                router(pe, NB - 2, 3)
                variance(pe, NB - 1)
                pointwise2(pe, NB - 1, 0)
                pointwise2(pe, NB - 1, 1)
                pointwise2(pe, NB - 1, 2)
                router(pe, NB - 1, 0)
                router(pe, NB - 1, 1)
                pointwise2(pe, NB - 1, 3)
                router(pe, NB - 1, 2)
                router(pe, NB - 1, 3)

            def squares_of_x(act, b):
                for i in range(TT):
                    act.wait_ge(x_in[i], 16 * (b + 1))
                    act.wait_ge(ss1_done, TT * b + i)
                    act.activation(junk[:, 0, :], xt[:, i, :], ACT.Square, accum_out=ss1[:, i:i + 1]).then_inc(ss1_done, 1)

            def scale_x(act, b):
                act.wait_ge(rstd1_done, b + 1)
                for i in range(TT):
                    act.activation(xt[:, i, :], xt[:, i, :], ACT.Copy, scale=r1[:, i:i + 1]).then_inc(xn_done, 1)

            def copy_h(act, b):
                for k in range(KD):
                    n = before_x(b)[k % 2] + k // 2
                    act.wait_ge(t_full[k % 2], n + 1)
                    act.activation(hT[:, k, :], ps_t[k % 2][:], ACT.Identity, bias=cols[:, k:k + 1],
                                   scale=cols[:, KD + k:KD + k + 1]).then_inc(t_free[k % 2], 1)

            def sigmoids(act, b, p):
                for cc in range(2):
                    ch = 2 * p + cc
                    act.wait_ge(g_full, KD * b + ch + 1)
                    if b or p:
                        act.wait_ge(glu_done, KD * b + ch - 1)
                    act.activation(sig[:, cc, :], ps_g[cc][:], ACT.Sigmoid,
                                   bias=vec[:, V_B1 + KD + ch:V_B1 + KD + ch + 1]).then_inc(sig_done, 1)

            def act_norm(act, q):
                for k in range(KD):
                    act.wait_ge(ln1_done, KD * q + k + 1)
                    act.wait_ge(sqsum_step, NSUM * q + (max(k - 3, 0) + 1 if k >= 2 else 0))
                    act.activation(sq[:, k % 2, :], s[:, k, :], ACT.Square).then_inc(sq_done, 1)
                if q:
                    copy_router(act, q - 1, 2)
                    copy_router(act, q - 1, 3)
                act.wait_ge(var_full, q + 1)
                act.wait_ge(ln2_done, KD * q)
                act.activation(rstd[:], ps_m[:], ACT.Sqrt, bias=eps_col[:]).then_inc(std_done, 1)

            def act_silu(act, q):
                for k in range(KD):
                    act.wait_ge(ln2_done, KD * q + k + 1)
                    act.activation(s[:, k, :], s[:, k, :], ACT.Silu, bias=vec[:, V_LB + k:V_LB + k + 1],
                                   scale=vec[:, V_LG + k:V_LG + k + 1]).then_inc(silu_done, 1)

            def copy_y(act, q, i):
                act.wait_ge(x1_out[i], 16 * q)
                act.wait_ge(h2_done, TT * q)
                for h in range(2):
                    act.wait_ge(y_full, 2 * TT * q + 2 * i + h + 1)
                    act.copy(ybuf[:, i, h * H:(h + 1) * H], ps_y[:]).then_inc(y_free, 1)

            def square_x1(act, q, i):
                act.wait_ge(x1_done, TT * q + i + 1)
                act.wait_ge(ms2_done, 2 * q)
                act.wait_ge(ss2_done, TT * q + i)
                act.activation(junk[:, 1, :], ybuf[:, i, :], ACT.Square, accum_out=ss2[:, i:i + 1]).then_inc(ss2_done, 1)

            def copy_router(act, q, i):
                n0, n1 = before_router(q, i)
                for t, n in ((0, n0), (1, n1)):
                    act.wait_ge(t_full[t], n + 1)
                    act.copy(h2T[:, 4 * t:4 * t + 4, :].rearrange("p k m -> p (k m)"), ps_t[t][:]).then_inc(t_free[t], 1)
                act.wait_ge(t_full[0], n0 + 2)
                act.copy(logits[:, q * TT + i, :], ps_t[0][:, 0:E]).then_inc(t_free[0], 1)

            def act_block(act, b, first=False, last=False):
                q = b - 1
                if not first:
                    act_norm(act, q)
                sigmoids(act, b, 1)
                if not first:
                    act_silu(act, q)
                sigmoids(act, b, 2)
                if not first:
                    copy_y(act, q, 0)
                if not last:
                    squares_of_x(act, b + 1)
                    scale_x(act, b + 1)
                sigmoids(act, b, 3)
                if not first:
                    copy_y(act, q, 1)
                    copy_y(act, q, 2)
                    square_x1(act, q, 0)
                    square_x1(act, q, 1)
                    copy_y(act, q, 3)
                if not last:
                    copy_h(act, b + 1)
                if not first:
                    for i in range(2, TT):
                        square_x1(act, q, i)
                if not last:
                    sigmoids(act, b + 1, 0)
                if not first:
                    copy_router(act, q, 0)
                    copy_router(act, q, 1)

            @block.scalar
            def _(act):
                act.wait_ge(pro_v, 1)
                act.activation(csil[:], vec[:, V_C:V_C + KD], ACT.Silu).then_inc(pro_a, 1)
                squares_of_x(act, 0)
                act.wait_ge(pro_v, 8)
                scale_x(act, 0)
                copy_h(act, 0)
                sigmoids(act, 0, 0)
                for b in range(NB):
                    act_block(act, b, first=b == 0, last=b == NB - 1)
                act_norm(act, NB - 1)
                act_silu(act, NB - 1)
                q = NB - 1
                copy_y(act, q, 0)
                copy_y(act, q, 1)
                square_x1(act, q, 0)
                square_x1(act, q, 1)
                copy_y(act, q, 2)
                copy_router(act, q, 0)
                copy_router(act, q, 1)
                square_x1(act, q, 2)
                copy_y(act, q, 3)
                square_x1(act, q, 3)
                copy_router(act, q, 2)
                copy_router(act, q, 3)

            def glu(dve, b, p):
                if b:
                    dve.wait_ge(hist_done, NP * b)
                for cc in range(2):
                    ch = 2 * p + cc
                    dve.wait_ge(sig_done, KD * b + ch + 1)
                    dve.wait_ge(a_full, KD * b + ch + 1)
                    dve.scalar_tensor_tensor(out=u[:, ch, HIST:], in0=ps_a[cc][:], scalar=vec[:, V_B1 + ch:V_B1 + ch + 1],
                                             in1=sig[:, cc, :], op0=ALU.add, op1=ALU.mult).then_inc(glu_done, 1)

            def taps(dve, b, p, j0, j1):
                for j in range(j0, j1):
                    for cc in range(2):
                        ch = 2 * p + cc
                        n = 2 * CW * (NP * b + p) + 2 * j + cc
                        if j == 0:
                            dve.wait_ge(glu_done, KD * b + ch + 1)
                            dve.tensor_scalar(v[:, ch, :], u[:, ch, 0:TB], wdw[:, ch, 0:1], vec[:, V_BDW + ch:V_BDW + ch + 1],
                                              ALU.mult, ALU.add).then_inc(tap_done, 1)
                        else:
                            dve.wait_ge(tap_done, n - 1)
                            dve.scalar_tensor_tensor(out=v[:, ch, :], in0=u[:, ch, j:j + TB], scalar=wdw[:, ch, j:j + 1],
                                                     in1=v[:, ch, :], op0=ALU.mult, op1=ALU.add).then_inc(tap_done, 1)
                if j1 == CW:
                    dve.wait_ge(tap_done, 2 * CW * (NP * b + p + 1))
                    chs = slice(2 * p, 2 * p + 2)
                    dve.tensor_copy(u[:, chs, 0:HIST], u[:, chs, TB:TB + HIST]).then_inc(hist_done, 1)

            def layer_norm1(dve, q):
                dve.wait_ge(mean_full, q + 1)
                dve.wait_ge(y_full, 2 * TT * q)
                for k in range(KD):
                    dve.tensor_tensor(s[:, k, :], v[:, k, :], ps_m[:], ALU.subtract).then_inc(ln1_done, 1)

            def layer_norm2(dve, q):
                dve.wait_ge(std_done, q + 1)
                dve.reciprocal(rstd[:], rstd[:]).then_inc(rstd_done, 1)
                dve.wait_ge(rstd_done, q + 1)
                for k in range(KD):
                    dve.tensor_tensor(s[:, k, :], s[:, k, :], rstd[:], ALU.mult).then_inc(ln2_done, 1)

            def residual(dve, q, i):
                dve.wait_ge(y_free, 2 * TT * q + 2 * i + 2)
                dve.wait_ge(xr_in[i % 2], 16 * (2 * q + i // 2 + 1))
                dve.tensor_tensor(ybuf[:, i, :], ybuf[:, i, :], xr[:, i % 2, :], ALU.add).then_inc(x1_done, 1)

            def second_norm(dve, q, i):
                dve.wait_ge(rstd2_done, 2 * q + i // 2 + 1)
                dve.wait_ge(h2_out[i % 2], 16 * (2 * q + i // 2))
                if i >= 2:
                    dve.wait_ge(t_full[1], before_router(q, i - 2)[1] + 1)
                elif q:
                    dve.wait_ge(t_full[1], before_router(q - 1, i + 2)[1] + 1)
                dve.scalar_tensor_tensor(out=h2[:, i % 2, :], in0=ybuf[:, i, :], scalar=r2[:, i:i + 1], in1=G2_row[:],
                                         op0=ALU.mult, op1=ALU.mult).then_inc(h2_half, 1)
                dve.wait_ge(h2_half, TT * q + i + 1)
                dve.tensor_tensor(h2[:, i % 2, :], h2[:, i % 2, :], sh2_row[:], ALU.add).then_inc(h2_done, 1)

            def dve_block(dve, b, first=False, last=False):
                q = b - 1
                if not first:
                    layer_norm1(dve, q)
                    dve.wait_ge(ln1_done, KD * b)
                taps(dve, b, 0, 0, 24)
                glu(dve, b, 1)
                taps(dve, b, 0, 24, CW)
                if not first:
                    layer_norm2(dve, q)
                taps(dve, b, 1, 0, 16)
                glu(dve, b, 2)
                taps(dve, b, 1, 16, CW)
                taps(dve, b, 2, 0, 16)
                glu(dve, b, 3)
                taps(dve, b, 2, 16, CW)
                if first:
                    taps(dve, b, 3, 0, CW)
                else:
                    residual(dve, q, 0)
                    residual(dve, q, 1)
                    taps(dve, b, 3, 0, 12)
                    second_norm(dve, q, 0)
                    second_norm(dve, q, 1)
                    taps(dve, b, 3, 12, 24)
                    residual(dve, q, 2)
                    residual(dve, q, 3)
                    taps(dve, b, 3, 24, CW)
                if not last:
                    glu(dve, b + 1, 0)
                if not first:
                    second_norm(dve, q, 2)
                    second_norm(dve, q, 3)

            @block.vector
            def _(dve):
                dve.memset(eps_col[:], EPS).then_inc(pro_a, 1)
                dve.wait_ge(pro_t, 1)
                dve.tensor_copy(vec[:], ps_t[0][:, 0:7 * KD]).then_inc(pro_v, 1)
                dve.wait_ge(pro_t, 2)
                dve.tensor_copy(wdw[:].rearrange("p k j -> p (k j)"), ps_t[1][:, 0:KD * CW]).then_inc(pro_v, 1)
                dve.wait_ge(pro_a, 2)
                dve.tensor_copy(csil_bc, csil[:].unsqueeze(2).to_broadcast([P, KD, P])).then_inc(pro_v, 1)
                for j in range(NPIECE):
                    dve.wait_ge(mods_full, j + 1)
                    dve.tensor_tensor(mod_rows[j // 2][:, (j % 2) * H:(j % 2 + 1) * H], ps_a[j % 2][:], bada[j % 2],
                                      ALU.add).then_inc(mods_row, 1)
                    if j == 3:
                        for n in range(4):
                            dve.wait_ge(pro_t, 3 + n)
                            dve.tensor_copy(cols[:, 4 * n:4 * n + 4],
                                            ps_g[0][:].rearrange("p (k m) -> p k m", k=4)[:, :, 0]).then_inc(pro_v, 1)
                        dve.wait_ge(pro_v, 7)
                        dve.scalar_tensor_tensor(out=cols[:, KD:], in0=cols[:, KD:], scalar=1.0, in1=vec[:, V_NG:V_NG + KD],
                                                 op0=ALU.add, op1=ALU.mult).then_inc(pro_v, 1)
                dve.wait_ge(mods_row, NPIECE)
                dve.wait_ge(vec_in, 160)
                dve.scalar_tensor_tensor(out=G2_row[:], in0=G2_row[:], scalar=1.0, in1=ng2_row, op0=ALU.add,
                                         op1=ALU.mult).then_inc(pro_v, 1)
                dve.tensor_tensor(b2_row, b2_row, g1_row, ALU.mult).then_inc(pro_v, 1)
                dve.wait_ge(pro_v, 10)
                dve.tensor_copy(gb_row[:], b2_row).then_inc(pro_v, 1)
                dve.wait_ge(pro_v, 11)
                dve.tensor_tensor(gb_row[LO:LO + 1, :], b2_row[LO:LO + 1, :], gb_row[LO:LO + 1, :].bitcast(F32),
                                  ALU.subtract).then_inc(pro_v, 1)
                dve.wait_ge(w2_in, 16)
                for k in range(KD):
                    dve.tensor_tensor(w2[:, k, :], w2[:, k, :], g1_row, ALU.mult).then_inc(pro_v, 1)
                dve.wait_ge(consts, 7)
                dve.tensor_copy(ones_hl[:], hl_f32).then_inc(pro_v, 1)
                dve.wait_ge(pro_v, 13 + KD)
                glu(dve, 0, 0)
                for b in range(NB):
                    dve_block(dve, b, first=b == 0, last=b == NB - 1)
                layer_norm1(dve, NB - 1)
                layer_norm2(dve, NB - 1)
                for i in (0, 2):
                    residual(dve, NB - 1, i)
                    residual(dve, NB - 1, i + 1)
                    second_norm(dve, NB - 1, i)
                    second_norm(dve, NB - 1, i + 1)

        moe = ExitStack()
        with moe:
            def mb(name, shape, dt=F32):
                return sb(name, shape, dt, moe)

            def ms(name):
                return sem(name, moe)

            NE = NT * E
            wi = mb("wi", [P, KD, 2 * DE])
            wo = mb("wo", [P, KE, D])
            wi_h, wi_l = mb("wi_h", [P, KD, 2 * DE], F32R), mb("wi_l", [P, KD, 2 * DE], F32R)
            wo_h, wo_l = mb("wo_h", [P, KE, D], F32R), mb("wo_l", [P, KE, D], F32R)
            xg = mb("xg", [P, D])
            xT_h, xT_l = mb("xT_h", [P, KD, P], F32R), mb("xT_l", [P, KD, P], F32R)
            gate = mb("gate", [P, DE])
            hid = mb("hid", [P, DE])
            hidT_h, hidT_l = mb("hidT_h", [P, KE, P], F32R), mb("hidT_l", [P, KE, P], F32R)
            ysb = mb("ysb", [P, D])
            rb = mb("rb", [P, E])
            ones = mb("ones", [P, P])
            below = mb("below", [P, P])
            pri = mb("pri", [P, E])
            thr = mb("thr", [P, NT])
            iota_p = mb("iota_p", [P, P])
            iota_t = mb("iota_t", [P, MTP])
            tokid = mb("tokid", [P, NT])
            zeros16 = mb("zeros16", [P, P], F16)
            scores = mb("scores", [P, NT, E])
            biased = mb("biased", [P, NT, E])
            tmp = mb("tmp", [P, NT, E])
            tmp2 = mb("tmp2", [P, NT, E])
            e1 = mb("e1", [P, NT, E])
            e2 = mb("e2", [P, NT, E])
            both = mb("both", [P, NT, E])
            cnt = mb("cnt", [P, NT, E])
            off = mb("off", [P, NT, E])
            gs = mb("gs", [P, NT, NG])
            gsel = mb("gsel", [P, NT, NG])
            tg = mb("tg", [P, NT, NG])
            mx = mb("mx", [P, NT])
            wts = mb("wts", [P, NT, 2])
            wsum = mb("wsum", [P, NT])
            total = mb("total", [P, E])
            ntile = mb("ntile", [P, E])
            cum = mb("cum", [P, E])
            base = mb("base", [P, E])
            onesE = mb("onesE", [P, E])
            cmp_t = mb("cmp_t", [P, MTP, E])
            slot_f = mb("slot_f", [P, 2, NT])
            slot_i = mb("slot_i", [P, 2, NT], I32)
            slot_hi = mb("slot_hi", [P, 2, NT], I32)
            slot_lo = mb("slot_lo", [P, 2, NT], I32)
            hi_f = mb("hi_f", [P, 2, NT])
            lo_f = mb("lo_f", [P, 2, NT])
            texp = mb("texp", [P, MTP])
            texp_i = mb("texp_i", [P, MTP], I32)
            fresh_f = mb("fresh_f", [P, MTP])
            fresh_i = mb("fresh_i", [P, MTP], I32)
            tok_i = mb("tok_i", [P, MTP], I32)
            sel_row = mb("sel_row", [P, 2, P], F16)
            sel_tile = mb("sel_tile", [P, 2, MTP], F16)
            idx = mb("idx", [P, 1], I32)
            cidx = mb("cidx", [P, NR, 2, 1], I32)
            wcol = mb("wcol", [P, NR, 2])
            ya, yb, x1r = wi[:, 0:NR, :], wi[:, NR:2 * NR, :], wo[:]

            ps_gate, ps_up, ps_t0, ps_t1, ps_h, ps_y0, ps_y1, ps_r = bank

            pool_pass = ms("pool_pass2")
            mconst, rb_in = ms("mconst"), ms("rb_in")
            sc_done, route, both_done, rank_full, sel_done, sel_used = ms("sc_done"), ms("route"), ms("both_done"), ms("rank_full"), ms("sel_done"), ms("sel_used")
            tok_full, lists = ms("tok_full"), ms("lists")
            idx_done, xg_in = ms("idx_done"), ms("xg_in")
            xp_full = [ms(f"xp_full{i}") for i in range(2)]
            xh_done, xl_done = [ms(f"xh_done{i}") for i in range(2)], [ms(f"xl_done{i}") for i in range(2)]
            wih_done, woh_done = ms("wih_done"), ms("woh_done")
            wil_dve, wil_pool, wol_dve, wol_pool = ms("wil_dve"), ms("wil_pool"), ms("wol_dve"), ms("wol_pool")
            wi_in = [ms(f"wi_in{k}") for k in range(KD)]
            wo_in = [ms(f"wo_in{k}") for k in range(KE)]
            g1_step, g2_step = ms("g1_step"), ms("g2_step")
            gate_done, hid_done, hp_full, hh_done, hl_done = ms("gate_done"), ms("hid_done"), ms("hp_full"), ms("hh_done"), ms("hl_done")
            y0_free, y1_free, y_out = ms("y0_free"), ms("y1_free"), ms("y_out")
            cidx_done, wcol_done = ms("cidx_done"), ms("wcol_done")
            ya_in = [ms(f"ya_in{i}") for i in range(NR)]
            yb_in = [ms(f"yb_in{i}") for i in range(NR)]
            x1_in = [ms(f"x1_in{i}") for i in range(NR)]
            ya_w, comb1, comb2 = ms("ya_w"), ms("comb1"), ms("comb2")
            comb3 = [ms(f"comb3_{i}") for i in range(NR)]
            out_done = [ms(f"out_done{i}") for i in range(NR)]

            out_rows = out.rearrange("o s d -> (o s) d")
            block = moe.enter_context(nc.Block())

            POOL_IN, POOL_OUT = (2, 5), (2,)

            def expert_of(eng, t):
                return 0 if isinstance(t, int) and t == 0 else eng.value_load(texp_i[0:1, bass.ds(t, 1)], min_val=0, max_val=E - 1)

            def first_of_expert(eng, t):
                return eng.value_load(fresh_i[0:1, bass.ds(t, 1)], min_val=0, max_val=1)

            def wait_lo(eng, what, e, k):
                pool_k, n, sem_pool, sem_dve = ((POOL_IN, KD, wil_pool, wil_dve) if what == "in" else
                                                (POOL_OUT, KE, wol_pool, wol_dve))
                mine = [j for j in range(n) if (j in pool_k) == (k in pool_k)]
                eng.wait_ge(sem_pool if k in pool_k else sem_dve, len(mine) * e + mine.index(k) + 1)

            def make_lo(eng, what, e, on_pool):
                for k in range(KD if what == "in" else KE):
                    if (k in (POOL_IN if what == "in" else POOL_OUT)) != on_pool:
                        continue
                    if what == "in":
                        eng.wait_ge(wih_done, KD * e + k + 1)
                        if on_pool:
                            eng.sem_inc(pool_pass, 1)
                        eng.tensor_tensor(wi_l[:, k, :], wi[:, k, :], wi_h[:, k, :].bitcast(F32), ALU.subtract).then_inc(
                            wil_pool if on_pool else wil_dve, 1)
                    else:
                        eng.wait_ge(woh_done, KE * e + k + 1)
                        if on_pool:
                            eng.sem_inc(pool_pass, 1)
                        eng.tensor_tensor(wo_l[:, k, :], wo[:, k, :], wo_h[:, k, :].bitcast(F32), ALU.subtract).then_inc(
                            wol_pool if on_pool else wol_dve, 1)

            def split_lo(eng, what, t, on_pool):
                with eng.If(first_of_expert(eng, t)):
                    make_lo(eng, what, expert_of(eng, t), on_pool)

            def make_hi(act, what, e, t, first=False):
                for k in range(KD if what == "in" else KE):
                    if what == "in":
                        if not first:
                            act.wait_ge(g1_step, KD * (t - 1) + k + 1)
                        act.wait_ge(wi_in[k], 16 * (e + 1))
                        act.copy(wi_h[:, k, :], wi[:, k, :]).then_inc(wih_done, 1)
                    else:
                        if not first:
                            act.wait_ge(g2_step, KE * (t - 1) + k + 1)
                        act.wait_ge(wo_in[k], 16 * (e + 1))
                        act.copy(wo_h[:, k, :], wo[:, k, :]).then_inc(woh_done, 1)

            def split_hi(act, what, t):
                with act.If(first_of_expert(act, t)):
                    make_hi(act, what, expert_of(act, t), t)

            def load_x1(sp, n):
                for j in range(NR):
                    sp.wait_ge(out_done[j], 16 * n)
                    sp.dma_start(x1r[:, j, :], x1_dram[bass.ds((NR * n + j) * P, P), :]).then_inc(x1_in[j], 16)

            def expert_in(e, k):
                return moe_w_in[0, bass.ds(e, 1), k * P:(k + 1) * P, :].rearrange("o p n -> (o p) n")

            def expert_out(e, k):
                return moe_w_out[0, bass.ds(e, 1), k * P:(k + 1) * P, :].rearrange("o p n -> (o p) n")

            def load_expert(sp, e, first=False):
                for k in range(KD):
                    if not first:
                        wait_lo(sp, "in", e - 1, k)
                    sp.dma_start(wi[:, k, :], expert_in(e, k)).then_inc(wi_in[k], 16)
                for k in range(KE):
                    if not first:
                        wait_lo(sp, "out", e - 1, k)
                    sp.dma_start(wo[:, k, :], expert_out(e, k)).then_inc(wo_in[k], 16)

            @block.sync
            def _(sp):
                sp.dma_start(rb[:], router_bias.rearrange("(o e) -> o e", o=1).to_broadcast([P, E])).then_inc(rb_in, 16)
                load_expert(sp, 0, first=True)
                with sp.Fori(1, E) as e:
                    load_expert(sp, e)
                for k in range(KE):
                    wait_lo(sp, "out", E - 1, k)
                load_x1(sp, 0)
                with sp.Fori(1, NT // NR) as n:
                    load_x1(sp, n)
                for j in range(NR):
                    sp.wait_ge(out_done[j], 16 * NT // NR)

            def gather_outputs(pool, n):
                for j in range(NR):
                    pool.wait_ge(comb3[j], n)
                    pool.wait_ge(ya_in[j], 16 * n)
                    pool.wait_ge(yb_in[j], 16 * n)
                    pool.sem_inc(pool_pass, 1)
                    for w in range(2):
                        pool.tensor_copy(cidx[:, j, w, :], slot_i[:, w, bass.ds(NR * n + j, 1)]).then_inc(cidx_done, 1)
                    pool.wait_ge(cidx_done, 2 * NR * n + 2 * j + 2)
                    pool.sem_inc(pool_pass, 1)
                    pool.indirect_dma_start(ya[:, j, :], None, y_dram[:, :], bass.IndirectOffsetOnAxis(ap=cidx[:, j, 0, :], axis=0)).then_inc(ya_in[j], 16)
                    pool.indirect_dma_start(yb[:, j, :], None, y_dram[:, :], bass.IndirectOffsetOnAxis(ap=cidx[:, j, 1, :], axis=0)).then_inc(yb_in[j], 16)

            def gather(pool, t, first=False):
                if not first:
                    pool.wait_ge(xg_in, 16 * t)
                pool.sem_inc(pool_pass, 1)
                pool.tensor_copy(idx[:], tok_i[:, bass.ds(t, 1)]).then_inc(idx_done, 1)
                if not first:
                    pool.wait_ge(xp_full[1], t)
                pool.wait_ge(idx_done, t + 1)
                pool.sem_inc(pool_pass, 1)
                pool.indirect_dma_start(xg[:], None, h2_dram[:, :], bass.IndirectOffsetOnAxis(ap=idx[:], axis=0)).then_inc(xg_in, 16)

            def pool_step(pool, t):
                split_lo(pool, "in", t + 2, on_pool=True)
                gather(pool, t + 3)
                split_lo(pool, "out", t + 1, on_pool=True)
                pool.sem_inc(pool_pass, 1)

            @block.gpsimd
            def _(pool):
                pool.memset(ones[:], 1.0).then_inc(mconst, 1)
                pool.memset(zeros16[:], 0.0).then_inc(mconst, 1)
                pool.memset(onesE[:], 1.0).then_inc(mconst, 1)
                pool.iota(pri[:], [[-1, E]], base=E, channel_multiplier=0, allow_small_or_imprecise_dtypes=True).then_inc(mconst, 1)
                pool.iota(thr[:], [[P, NT]], base=0, channel_multiplier=0, allow_small_or_imprecise_dtypes=True).then_inc(mconst, 1)
                pool.iota(iota_p[:], [[1, P]], base=0, channel_multiplier=0, allow_small_or_imprecise_dtypes=True).then_inc(mconst, 1)
                pool.iota(iota_t[:], [[1, MTP]], base=0, channel_multiplier=0, allow_small_or_imprecise_dtypes=True).then_inc(mconst, 1)
                pool.iota(tokid[:], [[P, NT]], base=0, channel_multiplier=1, allow_small_or_imprecise_dtypes=True).then_inc(mconst, 1)
                pool.wait_ge(mconst, 1)
                pool.affine_select(out=below[:], in_=ones[:], compare_op=ALU.is_gt, fill=0.0, base=0,
                                   pattern=[[1, P]], channel_multiplier=-1).then_inc(mconst, 1)
                make_lo(pool, "in", 0, on_pool=True)
                make_lo(pool, "out", 0, on_pool=True)
                pool.wait_ge(lists, 1)
                gather(pool, 0, first=True)
                gather(pool, 1)
                split_lo(pool, "in", 1, on_pool=True)
                gather(pool, 2)
                pool_step(pool, 0)
                with pool.Fori(1, MT - 3) as t:
                    pool_step(pool, t)
                split_lo(pool, "in", MT - 1, on_pool=True)
                pool.sem_inc(pool_pass, 1)
                split_lo(pool, "out", MT - 2, on_pool=True)
                pool.sem_inc(pool_pass, 1)
                split_lo(pool, "out", MT - 1, on_pool=True)
                for k in range(KD):
                    wait_lo(pool, "in", E - 1, k)
                pool.wait_ge(y_out, 16 * MT)
                gather_outputs(pool, 0)
                with pool.Fori(1, NT // NR) as n:
                    gather_outputs(pool, n)

            def transpose_rows(pe, t, first=False):
                pe.wait_ge(xg_in, 16 * (t + 1))
                for i, ps in enumerate((ps_t0, ps_t1)):
                    if not first:
                        pe.wait_ge(xh_done[i], t)
                        pe.wait_ge(xl_done[i], t)
                    for k in range(4):
                        at = (4 * i + k) * P
                        last = pe.transpose(ps[:, k * P:(k + 1) * P], xg[:, at:at + P], ident[:])
                    last.then_inc(xp_full[i], 1)

            def product(pe, ps, a_h, a_l, b_h, b_l, first, last):
                pe.matmul(ps, a_h, b_h, start=first, stop=False)
                pe.matmul(ps, a_h, b_l, start=False, stop=False)
                return pe.matmul(ps, a_l, b_h, start=False, stop=last)

            def ffn_in(pe, t, first=False):
                for i in range(2):
                    pe.wait_ge(xh_done[i], t + 1)
                    pe.wait_ge(xl_done[i], t + 1)
                if not first:
                    pe.wait_ge(hid_done, t)
                e = expert_of(pe, t)
                for k in range(KD):
                    pe.wait_ge(wih_done, KD * e + k + 1)
                    wait_lo(pe, "in", e, k)
                    product(pe, ps_gate[:], xT_h[:, k, :], xT_l[:, k, :], wi_h[:, k, 0:DE], wi_l[:, k, 0:DE],
                            k == 0, k == KD - 1)
                    product(pe, ps_up[:], xT_h[:, k, :], xT_l[:, k, :], wi_h[:, k, DE:2 * DE], wi_l[:, k, DE:2 * DE],
                            k == 0, k == KD - 1).then_inc(g1_step, 1)

            def transpose_hidden(pe, t):
                pe.wait_ge(hid_done, t + 1)
                pe.wait_ge(hh_done, t)
                pe.wait_ge(hl_done, t)
                for k in range(KE):
                    last = pe.transpose(ps_h[:, k * P:(k + 1) * P], hid[:, k * P:(k + 1) * P], ident[:])
                last.then_inc(hp_full, 1)

            def ffn_out(pe, t):
                pe.wait_ge(hh_done, t + 1)
                pe.wait_ge(hl_done, t + 1)
                pe.wait_ge(y0_free, t)
                pe.wait_ge(y1_free, t)
                e = expert_of(pe, t)
                for k in range(KE):
                    pe.wait_ge(woh_done, KE * e + k + 1)
                    wait_lo(pe, "out", e, k)
                    product(pe, ps_y0[:], hidT_h[:, k, :], hidT_l[:, k, :], wo_h[:, k, 0:H], wo_l[:, k, 0:H],
                            k == 0, k == KE - 1)
                    product(pe, ps_y1[:], hidT_h[:, k, :], hidT_l[:, k, :], wo_h[:, k, H:D], wo_l[:, k, H:D],
                            k == 0, k == KE - 1).then_inc(g2_step, 1)

            def pe_step(pe, t):
                transpose_hidden(pe, t)
                ffn_in(pe, t + 1)
                transpose_rows(pe, t + 2)
                ffn_out(pe, t)

            @block.tensor
            def _(pe):
                pe.wait_ge(mconst, 9)
                pe.wait_ge(both_done, 1)
                flat = both[:].rearrange("p t e -> p (t e)")
                pe.matmul(ps_t0[:, 0:NE], below[:], flat, start=True, stop=True)
                pe.matmul(ps_t1[:, 0:NE], ones[:], flat, start=True, stop=True).then_inc(rank_full, 1)
                pe.matmul(ps_r[:, 0:MTP], zeros16[:], zeros16[:, 0:MTP], start=True, stop=False, skip_group_check=True)
                with pe.Fori(0, NT) as i:
                    for w in range(2):
                        pe.wait_ge(sel_done, 4 * i + 2 * w + 2)
                        pe.matmul(ps_r[:, 0:MTP], sel_row[:, w, :], sel_tile[:, w, :], start=False, stop=False,
                                  skip_group_check=True).then_inc(sel_used, 1)
                pe.matmul(ps_r[:, 0:MTP], zeros16[:], zeros16[:, 0:MTP], start=False, stop=True,
                          skip_group_check=True).then_inc(tok_full, 1)
                pe.wait_ge(lists, 1)
                transpose_rows(pe, 0, first=True)
                ffn_in(pe, 0, first=True)
                transpose_rows(pe, 1)
                pe_step(pe, 0)
                with pe.Fori(1, MT - 2) as t:
                    pe_step(pe, t)
                transpose_hidden(pe, MT - 2)
                ffn_in(pe, MT - 1)
                ffn_out(pe, MT - 2)
                transpose_hidden(pe, MT - 1)
                ffn_out(pe, MT - 1)

            def copy_rows(act, t):
                for i, ps in enumerate((ps_t0, ps_t1)):
                    act.wait_ge(xp_full[i], t + 1)
                    act.copy(xT_h[:, 4 * i:4 * i + 4, :].rearrange("p k m -> p (k m)"), ps[:]).then_inc(xh_done[i], 1)

            def act_gate(act, t):
                act.wait_ge(g1_step, KD * (t + 1))
                act.wait_ge(hid_done, t)
                act.activation(gate[:], ps_gate[:], ACT.Silu).then_inc(gate_done, 1)

            def copy_hidden(act, t):
                act.wait_ge(hp_full, t + 1)
                act.copy(hidT_h[:].rearrange("p k m -> p (k m)"), ps_h[:]).then_inc(hh_done, 1)

            def copy_out(act, t):
                act.wait_ge(g2_step, KE * (t + 1))
                act.wait_ge(y_out, 16 * t)
                act.copy(ysb[:, 0:H], ps_y0[:]).then_inc(y0_free, 1)
                act.wait_ge(y0_free, t + 1)
                act.wait_ge(y1_free, t + 1)
                act.dma_start(y_dram[bass.ds(t * P, P), :], ysb[:]).then_inc(y_out, 16)

            def act_step(act, t):
                copy_hidden(act, t)
                split_hi(act, "in", t + 2)
                act_gate(act, t + 1)
                copy_rows(act, t + 2)
                split_hi(act, "out", t + 1)
                copy_out(act, t)

            def weigh(act, n):
                for j in range(NR):
                    act.wait_ge(ya_in[j], 16 * (n + 1))
                    act.wait_ge(wcol_done, NR * n + j + 1)
                    act.activation(ya[:, j, :], ya[:, j, :], ACT.Copy, scale=wcol[:, j, 0:1]).then_inc(ya_w, 1)
                for j in range(NR):
                    act.wait_ge(comb3[j], n + 1)
                    act.dma_start(out_rows[bass.ds((NR * n + j) * P, P), :], x1r[:, j, :]).then_inc(out_done[j], 16)

            @block.scalar
            def _(act):
                act.activation(scores[:], logits[:], ACT.Sigmoid).then_inc(sc_done, 1)
                make_hi(act, "in", 0, 0, first=True)
                make_hi(act, "out", 0, 0, first=True)
                act.wait_ge(lists, 1)
                copy_rows(act, 0)
                split_hi(act, "in", 1)
                act_gate(act, 0)
                copy_rows(act, 1)
                act_step(act, 0)
                with act.Fori(1, MT - 2) as t:
                    act_step(act, t)
                copy_hidden(act, MT - 2)
                act_gate(act, MT - 1)
                split_hi(act, "out", MT - 1)
                copy_out(act, MT - 2)
                copy_hidden(act, MT - 1)
                copy_out(act, MT - 1)
                weigh(act, 0)
                with act.Fori(1, NT // NR) as n:
                    weigh(act, n)

            def dve_step(dve, t):
                dve_hidden_lo(dve, t)
                split_lo(dve, "in", t + 2, on_pool=False)
                dve_hidden(dve, t + 1)
                dve_rows(dve, t + 2)
                split_lo(dve, "out", t + 1, on_pool=False)
                dve_out(dve, t)

            def combine(dve, n):
                for j in range(NR):
                    dve.wait_ge(comb1, NR * n)
                    dve.wait_ge(ya_w, NR * n)
                    dve.tensor_copy(wcol[:, j, :], wts[:, bass.ds(NR * n + j, 1), :].rearrange("p o w -> p (o w)")).then_inc(wcol_done, 1)
                for j in range(NR):
                    dve.wait_ge(ya_w, NR * n + j + 1)
                    dve.wait_ge(yb_in[j], 16 * (n + 1))
                    dve.wait_ge(wcol_done, NR * n + j + 1)
                    dve.scalar_tensor_tensor(out=ya[:, j, :], in0=yb[:, j, :], scalar=wcol[:, j, 1:2], in1=ya[:, j, :],
                                             op0=ALU.mult, op1=ALU.add).then_inc(comb1, 1)
                    dve.wait_ge(comb1, NR * n + j + 1)
                    dve.tensor_tensor(ya[:, j, :], ya[:, j, :], g2_row[:], ALU.mult).then_inc(comb2, 1)
                    dve.wait_ge(comb2, NR * n + j + 1)
                    dve.wait_ge(x1_in[j], 16 * (n + 1))
                    dve.tensor_tensor(x1r[:, j, :], ya[:, j, :], x1r[:, j, :], ALU.add).then_inc(comb3[j], 1)

            def one_hots(dve, i):
                for w in range(2):
                    dve.wait_ge(sel_used, 2 * i)
                    dve.tensor_scalar(sel_row[:, w, :], iota_p[:], lo_f[:, w, bass.ds(i, 1)], None, ALU.is_equal).then_inc(sel_done, 1)
                    dve.tensor_scalar(sel_tile[:, w, :], iota_t[:], hi_f[:, w, bass.ds(i, 1)], tokid[:, bass.ds(i, 1)],
                                      ALU.is_equal, ALU.mult).then_inc(sel_done, 1)

            def dve_rows(dve, t):
                for i, ps in enumerate((ps_t0, ps_t1)):
                    dve.wait_ge(xh_done[i], t + 1)
                    view = slice(4 * i, 4 * i + 4)
                    dve.tensor_tensor(xT_l[:, view, :].rearrange("p k m -> p (k m)"), ps[:],
                                      xT_h[:, view, :].bitcast(F32).rearrange("p k m -> p (k m)"), ALU.subtract).then_inc(xl_done[i], 1)

            def dve_hidden_lo(dve, t):
                dve.wait_ge(hh_done, t + 1)
                dve.tensor_tensor(hidT_l[:].rearrange("p k m -> p (k m)"), ps_h[:],
                                  hidT_h[:].bitcast(F32).rearrange("p k m -> p (k m)"), ALU.subtract).then_inc(hl_done, 1)

            def dve_hidden(dve, t):
                dve.wait_ge(gate_done, t + 1)
                dve.wait_ge(g1_step, KD * (t + 1))
                dve.wait_ge(hp_full, t)
                dve.tensor_tensor(hid[:], gate[:], ps_up[:], ALU.mult).then_inc(hid_done, 1)

            def dve_out(dve, t):
                dve.wait_ge(g2_step, KE * (t + 1))
                dve.wait_ge(y_out, 16 * t)
                dve.tensor_copy(ysb[:, H:D], ps_y1[:]).then_inc(y1_free, 1)

            @block.vector
            def _(dve):
                steps = [0]

                def then(ins):
                    steps[0] += 1
                    ins.then_inc(route, 1)
                    dve.wait_ge(route, steps[0])

                def bc_e(ap):
                    return ap.unsqueeze(2).to_broadcast([P, NT, E])

                def first_max(dst, src, t, n):
                    then(dve.tensor_reduce(mx[:], src, AX_X, ALU.max))
                    wide = mx[:].unsqueeze(2).to_broadcast([P, NT, n])
                    then(dve.tensor_tensor(t, src, wide, ALU.is_equal))
                    then(dve.tensor_tensor(t, t, pri[:, 0:n].unsqueeze(1).to_broadcast([P, NT, n]), ALU.mult))
                    then(dve.tensor_reduce(mx[:], t, AX_X, ALU.max))
                    then(dve.tensor_tensor(dst, t, wide, ALU.is_equal))

                dve.wait_ge(mconst, 9)
                dve.wait_ge(rb_in, 16)
                dve.wait_ge(sc_done, 1)
                then(dve.tensor_tensor(biased[:], scores[:], rb[:].unsqueeze(1).to_broadcast([P, NT, E]), ALU.add))
                bv = biased[:].rearrange("p t (g j) -> p (t g) j", j=EG)
                gflat, tflat = gs[:].rearrange("p t g -> p (t g)"), tg[:].rearrange("p t g -> p (t g)")
                pairs = [(i, j) for i in range(EG) for j in range(i + 1, EG)]
                for n, (i, j) in enumerate(pairs):
                    then(dve.tensor_tensor(gflat if n == 0 else tflat, bv[:, :, i], bv[:, :, j], ALU.add))
                    if n:
                        then(dve.tensor_tensor(gflat, gflat, tflat, ALU.max))
                first_max(gsel[:], gs[:], tg[:], NG)
                then(dve.tensor_scalar(tg[:], gsel[:], -1.0, BIG, ALU.add, ALU.mult))
                for j in range(EG):
                    view = biased[:].rearrange("p t (g j) -> p t g j", j=EG)[:, :, :, j]
                    then(dve.tensor_tensor(tmp2[:].rearrange("p t (g j) -> p t g j", j=EG)[:, :, :, j], view, tg[:], ALU.add))
                first_max(e1[:], tmp2[:], tmp[:], E)
                then(dve.scalar_tensor_tensor(out=tmp2[:].rearrange("p t e -> p (t e)"), in0=e1[:].rearrange("p t e -> p (t e)"),
                                              scalar=-3.0 * BIG, in1=tmp2[:].rearrange("p t e -> p (t e)"), op0=ALU.mult, op1=ALU.add))
                first_max(e2[:], tmp2[:], tmp[:], E)
                dve.tensor_tensor(both[:], e1[:], e2[:], ALU.add).then_inc(both_done, 1)
                for w, e in enumerate((e1, e2)):
                    then(dve.tensor_tensor(tmp[:], e[:], scores[:], ALU.mult))
                    then(dve.tensor_reduce(wts[:, :, w], tmp[:], AX_X, ALU.add))
                then(dve.tensor_tensor(wsum[:], wts[:, :, 0], wts[:, :, 1], ALU.add))
                then(dve.reciprocal(wsum[:], wsum[:]))
                then(dve.tensor_tensor(wts[:], wts[:], wsum[:].unsqueeze(2).to_broadcast([P, NT, 2]), ALU.mult))
                dve.wait_ge(rank_full, 1)
                then(dve.tensor_copy(cnt[:].rearrange("p t e -> p (t e)"), ps_t1[:, 0:NE]))
                then(dve.memset(off[:, 0, :], 0.0))
                for t in range(1, NT):
                    then(dve.tensor_tensor(off[:, t, :], off[:, t - 1, :], cnt[:, t - 1, :], ALU.add))
                then(dve.tensor_tensor(total[:], off[:, NT - 1, :], cnt[:, NT - 1, :], ALU.add))
                ct = cmp_t[:, 0:E, :].rearrange("p e k -> p e k")
                then(dve.tensor_tensor(ct[:, :, 0:NT], total[:].unsqueeze(2).to_broadcast([P, E, NT]),
                                       thr[:].unsqueeze(1).to_broadcast([P, E, NT]), ALU.is_gt))
                then(dve.tensor_reduce(ntile[:], ct[:, :, 0:NT], AX_X, ALU.add))
                then(dve.tensor_scalar(ntile[:], ntile[:], 1.0, None, ALU.max))
                then(dve.tensor_tensor_scan(cum[:], onesE[:], ntile[:], 0.0, ALU.mult, ALU.add))
                then(dve.tensor_tensor(base[:], cum[:], ntile[:], ALU.subtract))
                then(dve.tensor_scalar(base[:], base[:], float(P), None, ALU.mult))
                then(dve.tensor_tensor(cmp_t[:], cum[:].unsqueeze(1).to_broadcast([P, MTP, E]),
                                       iota_t[:].unsqueeze(2).to_broadcast([P, MTP, E]), ALU.is_le))
                then(dve.tensor_reduce(texp[:], cmp_t[:], AX_X, ALU.add))
                then(dve.tensor_scalar(texp[:], texp[:], float(E - 1), None, ALU.min))
                then(dve.tensor_copy(texp_i[:], texp[:]))
                then(dve.memset(fresh_f[:], 1.0))
                then(dve.tensor_tensor(fresh_f[:, 1:MTP], texp[:, 1:MTP], texp[:, 0:MT], ALU.not_equal))
                then(dve.tensor_copy(fresh_i[:], fresh_f[:]))
                then(dve.tensor_tensor(off[:].rearrange("p t e -> p (t e)"), off[:].rearrange("p t e -> p (t e)"), ps_t0[:, 0:NE], ALU.add))
                then(dve.tensor_tensor(off[:], off[:], base[:].unsqueeze(1).to_broadcast([P, NT, E]), ALU.add))
                for w, e in enumerate((e1, e2)):
                    then(dve.tensor_tensor(tmp[:], e[:], off[:], ALU.mult))
                    then(dve.tensor_reduce(slot_f[:, w, :], tmp[:], AX_X, ALU.add))
                then(dve.tensor_copy(slot_i[:], slot_f[:]))
                then(dve.tensor_scalar(slot_hi[:], slot_i[:], 7, None, ALU.arith_shift_right))
                then(dve.tensor_scalar(slot_lo[:], slot_i[:], P - 1, None, ALU.bitwise_and))
                then(dve.tensor_copy(hi_f[:], slot_hi[:]))
                then(dve.tensor_copy(lo_f[:], slot_lo[:]))
                one_hots(dve, 0)
                with dve.Fori(1, NT) as i:
                    one_hots(dve, i)
                dve.wait_ge(tok_full, 1)
                dve.tensor_copy(tok_i[:], ps_r[:, 0:MTP]).then_inc(lists, 1)
                make_lo(dve, "in", 0, on_pool=False)
                dve_rows(dve, 0)
                make_lo(dve, "out", 0, on_pool=False)
                dve.wait_ge(lists, 1)
                split_lo(dve, "in", 1, on_pool=False)
                dve_hidden(dve, 0)
                dve_rows(dve, 1)
                dve_step(dve, 0)
                with dve.Fori(1, MT - 2) as t:
                    dve_step(dve, t)
                dve_hidden_lo(dve, MT - 2)
                dve_hidden(dve, MT - 1)
                split_lo(dve, "out", MT - 1, on_pool=False)
                dve_out(dve, MT - 2)
                dve_hidden_lo(dve, MT - 1)
                dve_out(dve, MT - 1)
                combine(dve, 0)
                with dve.Fori(1, NT // NR) as n:
                    combine(dve, n)

_INS = ['x', 'c', 'norm_mix_g', 'norm_ffn_g', 'w_ada', 'b_ada', 'conv_w_pw1', 'conv_b_pw1', 'conv_w_dw', 'conv_b_dw',
        'conv_ln_g', 'conv_ln_b', 'conv_w_pw2', 'conv_b_pw2', 'router_w', 'router_bias', 'moe_w_in', 'moe_w_out']


def kernel(**inputs):
    import numpy as _np
    import concourse.bacc as _bacc
    from concourse import mybir as _mybir
    from concourse.bass_utils import run_bass_kernel_spmd as _run

    nc = _bacc.Bacc("TRN2", target_bir_lowering=False, num_devices=1)
    arrays, args = {}, []
    for name in _INS:
        a = _np.ascontiguousarray(inputs[name])
        arrays[f"in_{name}_dram"] = a
        args.append(nc.dram_tensor(f"in_{name}_dram", a.shape, _mybir.dt.from_np(a.dtype), kind="ExternalInput").ap())
    shape = tuple(inputs["x"].shape)
    out = nc.dram_tensor("out_0_dram", shape, _mybir.dt.float32, kind="ExternalOutput").ap()
    kernel_program(nc, *args, out)
    r = _run(nc, [arrays], core_ids=[0])
    return r.results[0]["out_0_dram"]
```
